# Optimizing a Trainium2 kernel written in Bass

```python
import math
import jax
import jax.numpy as jnp
from jax import lax
import numpy as np

D_MODEL = 1024
BATCH = 1
SEQ = 512
DEPTH = 2
DEC_BATCH = 8
DEC_SEQ = 1
PAST_LEN = 4096
PAGE_SIZE = 128

N_META = 16
EPS = 1e-6
H_A = 8
DK_A = 64
DV_A = 64
CONV_W = 4
CHUNK_A = 64
H_B = 8
DH_B = 64
H_IDX = 8
D_IDX = 64
TOPK_MAX = 256
REL_BUCKETS = 32
REL_MAX_DIST = 1024
H_C = 8
Q_LORA = 384
KV_LORA = 256
QK_NOPE = 64
QK_ROPE = 32
V_C = 128
ROPE_BASE = 10000.0
D_FF = 4 * D_MODEL
Q_BLOCK = 128

QKV_A = H_A * (2 * DK_A + DV_A)
AB_SIZES = (QKV_A, H_A, H_A, H_A * DV_A, H_B * DH_B, H_B * DH_B, H_B * DH_B, H_IDX * D_IDX, H_IDX, D_IDX)
AB_COLS = sum(AB_SIZES)
C_SIZES = (Q_LORA, KV_LORA, QK_ROPE)
C_COLS = sum(C_SIZES)
MLA_SCALE = (QK_NOPE + QK_ROPE) ** -0.5
N_AB = (DEPTH + 1) // 2
N_C = DEPTH // 2

kernel_name = 'hybrid_gdn_dsa_mla_step'

def rmsnorm(x, w):
    xf = x.astype(jnp.float32)
    y = xf * lax.rsqrt(jnp.mean(xf * xf, axis=-1, keepdims=True) + EPS)
    return (y * w.astype(jnp.float32)).astype(x.dtype)

def l2norm(x):
    return x * lax.rsqrt(jnp.sum(x * x, axis=-1, keepdims=True) + EPS)

def split_cols(x, sizes):
    out, off = [], 0
    for s in sizes:
        out.append(x[..., off:off + s])
        off += s
    return out

def to_blocks(a, n_blocks):
    b, t = a.shape[:2]
    pad = n_blocks * Q_BLOCK - t
    a = jnp.pad(a, [(0, 0), (0, pad)] + [(0, 0)] * (a.ndim - 2))
    return jnp.moveaxis(a.reshape((b, n_blocks, Q_BLOCK) + a.shape[2:]), 1, 0)

def from_blocks(a, t):
    a = jnp.moveaxis(a, 0, 1)
    return a.reshape((a.shape[0], -1) + a.shape[3:])[:, :t]

def gather_pages(pool, page_table):
    g = pool[page_table]
    return g.reshape((g.shape[0], g.shape[1] * g.shape[2]) + g.shape[3:])

def gather_rows(pool, page_table, idx):
    db = idx.shape[0]
    page = idx // PAGE_SIZE
    off = idx % PAGE_SIZE
    phys = jnp.take_along_axis(page_table, page.reshape(db, -1), axis=1).reshape(idx.shape)
    return pool[phys, off]

def rel_bucket(dist):
    dist = jnp.maximum(dist, 0)
    max_exact = REL_BUCKETS // 2
    log_ratio = jnp.log(jnp.maximum(dist, 1).astype(jnp.float32) / max_exact) / math.log(REL_MAX_DIST / max_exact)
    large = max_exact + (log_ratio * (REL_BUCKETS - max_exact)).astype(jnp.int32)
    return jnp.where(dist < max_exact, dist, jnp.minimum(large, REL_BUCKETS - 1))

def rope(x, pos):
    half = QK_ROPE // 2
    inv = ROPE_BASE ** (-jnp.arange(half, dtype=jnp.float32) / half)
    ang = pos.astype(jnp.float32)[:, None] * inv[None, :]
    cos = jnp.cos(ang)[:, None, :]
    sin = jnp.sin(ang)[:, None, :]
    xf = x.astype(jnp.float32)
    x1, x2 = xf[..., :half], xf[..., half:]
    return jnp.concatenate([x1 * cos - x2 * sin, x2 * cos + x1 * sin], axis=-1).astype(x.dtype)

def causal_conv(xp, w, t):
    acc = xp[:, 0:t] * w[0]
    for j in range(1, CONV_W):
        acc = acc + xp[:, j:j + t] * w[j]
    return jax.nn.silu(acc)

def sq_relu_mlp(x, w_up, w_down):
    return jnp.square(jax.nn.relu(x @ w_up)) @ w_down

def gdn_prep(qkv, alpha, braw, a_log, dt_bias):
    b, t = qkv.shape[:2]
    qkv = qkv.astype(jnp.float32)
    q, k, v = split_cols(qkv, (H_A * DK_A, H_A * DK_A, H_A * DV_A))
    q = l2norm(q.reshape(b, t, H_A, DK_A)) * DK_A ** -0.5
    k = l2norm(k.reshape(b, t, H_A, DK_A))
    v = v.reshape(b, t, H_A, DV_A)
    g = -jnp.exp(a_log.astype(jnp.float32)) * jax.nn.softplus(alpha.astype(jnp.float32) + dt_bias.astype(jnp.float32))
    beta = jax.nn.sigmoid(braw.astype(jnp.float32))
    return q, k, v, g, beta

def gdn_chunk(s, q, k, v, g, beta):
    c = q.shape[2]
    gcum = jnp.cumsum(g, axis=-1)
    incl = jnp.tril(jnp.ones((c, c), dtype=bool))
    strict = jnp.tril(jnp.ones((c, c), dtype=bool), -1)
    decay = jnp.exp(jnp.where(incl, gcum[..., :, None] - gcum[..., None, :], -jnp.inf))
    kk = jnp.einsum('bhid,bhjd->bhij', k, k)
    a_mat = jnp.where(strict, beta[..., :, None] * kk * decay, 0.0) + jnp.eye(c, dtype=q.dtype)
    rhs = jnp.concatenate([v * beta[..., None], k * (beta * jnp.exp(gcum))[..., None]], axis=-1)
    sol = lax.linalg.triangular_solve(a_mat, rhs, left_side=True, lower=True, unit_diagonal=True)
    u, w = sol[..., :DV_A], sol[..., DV_A:]
    v_new = u - jnp.einsum('bhck,bhkv->bhcv', w, s)
    qk = jnp.einsum('bhid,bhjd->bhij', q, k) * decay
    o = jnp.einsum('bhck,bhkv->bhcv', q * jnp.exp(gcum)[..., None], s) + jnp.einsum('bhij,bhjv->bhiv', qk, v_new)
    g_last = gcum[..., -1:]
    s_new = s * jnp.exp(g_last)[..., None] + jnp.einsum('bhck,bhcv->bhkv', k * jnp.exp(g_last - gcum)[..., None], v_new)
    return s_new, o

def gdn_step(s, xs):
    q, k, v, g, beta = xs
    s = s * jnp.exp(g)[..., None, None]
    delta = (v - jnp.einsum('bhk,bhkv->bhv', k, s)) * beta[..., None]
    s = s + jnp.einsum('bhk,bhv->bhkv', k, delta)
    return s, jnp.einsum('bhk,bhkv->bhv', q, s)

def gdn_prompt(q, k, v, g, beta):
    b, t = q.shape[:2]
    q, k, v, g, beta = (jnp.moveaxis(a, 1, 2) for a in (q, k, v, g, beta))
    s0 = jnp.zeros((b, H_A, DK_A, DV_A), jnp.float32)
    s1, o_meta = gdn_chunk(s0, q[:, :, :N_META], k[:, :, :N_META], v[:, :, :N_META], g[:, :, :N_META], beta[:, :, :N_META])
    n_chunks = (t - N_META) // CHUNK_A

    def to_chunks(a):
        a = a[:, :, N_META:]
        a = a.reshape(a.shape[:2] + (n_chunks, CHUNK_A) + a.shape[3:])
        return jnp.moveaxis(a, 2, 0)

    s_fin, o_chunks = lax.scan(lambda s, xs: gdn_chunk(s, *xs), s1, tuple(to_chunks(a) for a in (q, k, v, g, beta)))
    o_real = jnp.moveaxis(o_chunks, 0, 2).reshape(b, H_A, n_chunks * CHUNK_A, DV_A)
    o = jnp.concatenate([o_meta, o_real], axis=2)
    return jnp.moveaxis(o, 1, 2), s_fin

def gdn_decode(s, q, k, v, g, beta):
    xs = tuple(jnp.moveaxis(a, 1, 0) for a in (q, k, v, g, beta))
    s_fin, o = lax.scan(gdn_step, s.astype(jnp.float32), xs)
    return jnp.moveaxis(o, 0, 1), s_fin

def index_scores(qi, wi, ki):
    s = jax.nn.relu(jnp.einsum('bthd,bsd->bths', qi, ki).astype(jnp.float32) * D_IDX ** -0.5)
    return jnp.einsum('bths,bth->bts', s, wi.astype(jnp.float32) * H_IDX ** -0.5)

def sparse_attend(q, k_sel, v_sel, valid, dist, rel_bias):
    logits = jnp.einsum('bthd,btkhd->bthk', q, k_sel).astype(jnp.float32) * DH_B ** -0.5
    bias = rel_bias[rel_bucket(dist)]
    logits = logits + jnp.moveaxis(bias, -1, -2).astype(jnp.float32)
    logits = jnp.where(valid[:, :, None, :], logits, -jnp.inf)
    p = jax.nn.softmax(logits, axis=-1).astype(v_sel.dtype)
    return jnp.einsum('bthk,btkhd->bthd', p, v_sel)

def gather_seq(rows, idx):
    return jax.vmap(lambda rb, ib: rb[ib])(rows, idx)

def dsa_prompt(q, k, v, qi, wi, ki, rel_bias):
    b, t = q.shape[:2]
    topk = min(TOPK_MAX, SEQ // 4)
    nb = -(-t // Q_BLOCK)
    pos_blocks = jnp.arange(nb * Q_BLOCK, dtype=jnp.int32).reshape(nb, Q_BLOCK)
    key_pos = jnp.arange(t, dtype=jnp.int32)

    def one_block(xs):
        qb, qib, wib, pos = xs
        sc = index_scores(qib, wib, ki)
        sc = jnp.where((key_pos[None, :] <= pos[:, None])[None], sc, -jnp.inf)
        _, idx = lax.top_k(sc, topk)
        valid = idx <= pos[None, :, None]
        dist = pos[None, :, None] - idx
        return sparse_attend(qb, gather_seq(k, idx), gather_seq(v, idx), valid, dist, rel_bias)

    o = lax.map(one_block, (to_blocks(q, nb), to_blocks(qi, nb), to_blocks(wi, nb), pos_blocks))
    return from_blocks(o, t)

def dsa_decode(q, k_new, v_new, qi, wi, ki_new, cache_k, cache_v, cache_ki, page_table, rel_bias):
    db, t = q.shape[:2]
    n_keys = PAST_LEN + t
    topk = min(TOPK_MAX, n_keys // 4)
    ki_all = jnp.concatenate([gather_pages(cache_ki, page_table).astype(ki_new.dtype), ki_new], axis=1)
    pos = PAST_LEN + jnp.arange(t, dtype=jnp.int32)
    sc = index_scores(qi, wi, ki_all)
    key_pos = jnp.arange(n_keys, dtype=jnp.int32)
    sc = jnp.where((key_pos[None, :] <= pos[:, None])[None], sc, -jnp.inf)
    _, idx = lax.top_k(sc, topk)
    valid = idx <= pos[None, :, None]
    in_past = (idx < PAST_LEN)[..., None, None]
    past_idx = jnp.minimum(idx, PAST_LEN - 1)
    new_idx = jnp.clip(idx - PAST_LEN, 0, t - 1)
    k_sel = jnp.where(in_past, gather_rows(cache_k, page_table, past_idx).astype(k_new.dtype), gather_seq(k_new, new_idx))
    v_sel = jnp.where(in_past, gather_rows(cache_v, page_table, past_idx).astype(v_new.dtype), gather_seq(v_new, new_idx))
    dist = pos[None, :, None] - idx
    return sparse_attend(q, k_sel, v_sel, valid, dist, rel_bias)

def mixer_ab(hn, w_in, conv_w, a_log, dt_bias, gnorm, w_out, rel_bias, past):
    b, t, _ = hn.shape
    qkv_a, alpha, braw, gate, q_b, k_b, v_b, qi, wi, ki = split_cols(hn @ w_in, AB_SIZES)
    if past is None:
        conv_buf = jnp.zeros((b, CONV_W - 1, QKV_A), qkv_a.dtype)
    else:
        conv_buf, s_prev, cache_k, cache_v, cache_ki, page_table = past
    xp = jnp.concatenate([conv_buf.astype(qkv_a.dtype), qkv_a], axis=1)
    q, k, v, g, beta = gdn_prep(causal_conv(xp, conv_w, t), alpha, braw, a_log, dt_bias)
    if past is None:
        o_a, s_new = gdn_prompt(q, k, v, g, beta)
    else:
        o_a, s_new = gdn_decode(s_prev, q, k, v, g, beta)
    o_a = rmsnorm(o_a, gnorm) * jax.nn.silu(gate.reshape(b, t, H_A, DV_A).astype(jnp.float32))
    o_a = o_a.reshape(b, t, H_A * DV_A).astype(hn.dtype)
    q_b = q_b.reshape(b, t, H_B, DH_B)
    k_b = k_b.reshape(b, t, H_B, DH_B)
    v_b = v_b.reshape(b, t, H_B, DH_B)
    qi = qi.reshape(b, t, H_IDX, D_IDX)
    if past is None:
        o_b = dsa_prompt(q_b, k_b, v_b, qi, wi, ki, rel_bias)
    else:
        o_b = dsa_decode(q_b, k_b, v_b, qi, wi, ki, cache_k, cache_v, cache_ki, page_table, rel_bias)
    out = jnp.concatenate([o_a, o_b.reshape(b, t, H_B * DH_B).astype(hn.dtype)], axis=-1) @ w_out
    return out, (xp[:, -(CONV_W - 1):], s_new, k_b, v_b, ki)

def mla_core(q_lat, q_pe, c, kpe, visible):
    logits = (jnp.einsum('bthc,bsc->bhts', q_lat, c) + jnp.einsum('bthr,bsr->bhts', q_pe, kpe)).astype(jnp.float32) * MLA_SCALE
    logits = jnp.where(visible[None, None], logits, -jnp.inf)
    p = jax.nn.softmax(logits, axis=-1).astype(c.dtype)
    return jnp.einsum('bhts,bsc->bthc', p, c)

def mla_prompt(q_lat, q_pe, c, kpe):
    t = q_lat.shape[1]
    nb = -(-t // Q_BLOCK)
    pos_blocks = jnp.arange(nb * Q_BLOCK, dtype=jnp.int32).reshape(nb, Q_BLOCK)
    key_pos = jnp.arange(t, dtype=jnp.int32)

    def one_block(xs):
        ql, qp, pos = xs
        return mla_core(ql, qp, c, kpe, key_pos[None, :] <= pos[:, None])

    o = lax.map(one_block, (to_blocks(q_lat, nb), to_blocks(q_pe, nb), pos_blocks))
    return from_blocks(o, t)

def mixer_c(hn, w_in, qnorm, kvnorm, w_uq, w_uk, w_uv, w_out, past):
    b, t, _ = hn.shape
    cq, ckv, kpe = split_cols(hn @ w_in, C_SIZES)
    offset = 0 if past is None else PAST_LEN
    pos = offset + jnp.arange(t, dtype=jnp.int32)
    qf = (rmsnorm(cq, qnorm) @ w_uq).reshape(b, t, H_C, QK_NOPE + QK_ROPE)
    q_pe = rope(qf[..., QK_NOPE:], pos)
    q_lat = jnp.einsum('bthn,chn->bthc', qf[..., :QK_NOPE], w_uk)
    c = rmsnorm(ckv, kvnorm)
    kpe = rope(kpe[:, :, None, :], pos)[:, :, 0, :]
    if past is None:
        o_lat = mla_prompt(q_lat, q_pe, c, kpe)
    else:
        cache_c, cache_kpe, page_table = past
        c_all = jnp.concatenate([gather_pages(cache_c, page_table).astype(c.dtype), c], axis=1)
        kpe_all = jnp.concatenate([gather_pages(cache_kpe, page_table).astype(kpe.dtype), kpe], axis=1)
        key_pos = jnp.arange(PAST_LEN + t, dtype=jnp.int32)
        o_lat = mla_core(q_lat, q_pe, c_all, kpe_all, key_pos[None, :] <= pos[:, None])
    o = jnp.einsum('bthc,chv->bthv', o_lat, w_uv).reshape(b, t, H_C * V_C)
    return o @ w_out, (c, kpe)

def setup_inputs(seed: int = 0) -> dict:
    key = jax.random.key(seed)
    keys = list(jax.random.split(key, 40))

    def nrm(shape, scale=1.0):
        return jax.random.normal(keys.pop(), shape, jnp.float32) * scale

    def gain(shape):
        return 1.0 + nrm(shape, 0.01)

    n_pages = PAST_LEN // PAGE_SIZE
    n_used = DEC_BATCH * n_pages
    n_pool = n_used + n_used // 4
    page_table = jax.random.permutation(keys.pop(), n_pool)[:n_used].reshape(DEC_BATCH, n_pages).astype(jnp.int32)
    dt = jnp.exp(jax.random.uniform(keys.pop(), (N_AB, H_A), jnp.float32, math.log(1e-3), math.log(1e-1)))
    dt_bias_a = dt + jnp.log(-jnp.expm1(-dt))
    a_log = jnp.log(jax.random.uniform(keys.pop(), (N_AB, H_A), jnp.float32, 1.0, 16.0))
    return {
        'x_prompt': nrm((BATCH, SEQ, D_MODEL)),
        'x_sample': nrm((DEC_BATCH, DEC_SEQ, D_MODEL)),
        'state_a_conv': nrm((N_AB, DEC_BATCH, CONV_W - 1, QKV_A)),
        'state_a_ssm': nrm((N_AB, DEC_BATCH, H_A, DK_A, DV_A), 0.1),
        'cache_b_k': nrm((N_AB, n_pool, PAGE_SIZE, H_B, DH_B)),
        'cache_b_v': nrm((N_AB, n_pool, PAGE_SIZE, H_B, DH_B)),
        'cache_b_kidx': nrm((N_AB, n_pool, PAGE_SIZE, D_IDX)),
        'cache_c_latent': nrm((N_C, n_pool, PAGE_SIZE, KV_LORA)),
        'cache_c_kpe': nrm((N_C, n_pool, PAGE_SIZE, QK_ROPE)),
        'page_table': page_table,
        'meta_tokens': nrm((N_META, D_MODEL)),
        'rel_bias': nrm((REL_BUCKETS, H_B), 0.5),
        'norm_mix': gain((DEPTH, D_MODEL)),
        'norm_ffn': gain((DEPTH, D_MODEL)),
        'norm_final': gain((D_MODEL,)),
        'w_in_ab': nrm((N_AB, D_MODEL, AB_COLS), D_MODEL ** -0.5),
        'conv_a': nrm((N_AB, CONV_W, QKV_A), CONV_W ** -0.5),
        'a_log': a_log,
        'dt_bias_a': dt_bias_a,
        'gnorm_a': gain((N_AB, DV_A)),
        'w_out_ab': nrm((N_AB, H_A * DV_A + H_B * DH_B, D_MODEL), (H_A * DV_A + H_B * DH_B) ** -0.5),
        'w_in_c': nrm((N_C, D_MODEL, C_COLS), D_MODEL ** -0.5),
        'qnorm_c': gain((N_C, Q_LORA)),
        'kvnorm_c': gain((N_C, KV_LORA)),
        'w_uq_c': nrm((N_C, Q_LORA, H_C * (QK_NOPE + QK_ROPE)), Q_LORA ** -0.5),
        'w_uk_c': nrm((N_C, KV_LORA, H_C, QK_NOPE), KV_LORA ** -0.5),
        'w_uv_c': nrm((N_C, KV_LORA, H_C, V_C), KV_LORA ** -0.5),
        'w_out_c': nrm((N_C, H_C * V_C, D_MODEL), (H_C * V_C) ** -0.5),
        'w_up': nrm((DEPTH, D_MODEL, D_FF), D_MODEL ** -0.5),
        'w_down': nrm((DEPTH, D_FF, D_MODEL), D_FF ** -0.5),
    }

def reference(x_prompt, x_sample, state_a_conv, state_a_ssm, cache_b_k, cache_b_v, cache_b_kidx,
              cache_c_latent, cache_c_kpe, page_table, meta_tokens, rel_bias, norm_mix, norm_ffn, norm_final,
              w_in_ab, conv_a, a_log, dt_bias_a, gnorm_a, w_out_ab, w_in_c, qnorm_c, kvnorm_c,
              w_uq_c, w_uk_c, w_uv_c, w_out_c, w_up, w_down):

    def trunk(h, sample):
        ab_states, c_states = [], []
        for li in range(DEPTH):
            j = li // 2
            hn = rmsnorm(h, norm_mix[li])
            if li % 2 == 0:
                past = (state_a_conv[j], state_a_ssm[j], cache_b_k[j], cache_b_v[j], cache_b_kidx[j], page_table) if sample else None
                out, st = mixer_ab(hn, w_in_ab[j], conv_a[j], a_log[j], dt_bias_a[j], gnorm_a[j], w_out_ab[j], rel_bias, past)
                ab_states.append(st)
            else:
                past = (cache_c_latent[j], cache_c_kpe[j], page_table) if sample else None
                out, st = mixer_c(hn, w_in_c[j], qnorm_c[j], kvnorm_c[j], w_uq_c[j], w_uk_c[j], w_uv_c[j], w_out_c[j], past)
                c_states.append(st)
            h = h + out.astype(h.dtype)
            h = h + sq_relu_mlp(rmsnorm(h, norm_ffn[li]), w_up[li], w_down[li]).astype(h.dtype)
        y = rmsnorm(h, norm_final)
        ab = [jnp.stack(z) for z in zip(*ab_states)]
        cc = [jnp.stack(z) for z in zip(*c_states)]
        return y, ab, cc

    meta = jnp.broadcast_to(meta_tokens[None].astype(x_prompt.dtype), (x_prompt.shape[0], N_META, D_MODEL))
    y_p, ab_p, c_p = trunk(jnp.concatenate([meta, x_prompt], axis=1), False)
    y_s, ab_s, c_s = trunk(x_sample, True)
    return (y_p[:, N_META:], y_s,
            ab_p[0], ab_p[1], ab_p[2], ab_p[3], ab_p[4], c_p[0], c_p[1],
            ab_s[0], ab_s[1], ab_s[2], ab_s[3], ab_s[4], c_s[0], c_s[1])


_drawn_inputs = setup_inputs


def setup_inputs(seed=0):
    import zlib

    import numpy as np

    out = dict(_drawn_inputs(seed))
    spreads = {}
    factors = {'cache_c_latent': 3.385,
     'cache_c_kpe': 16.659,
     'norm_mix': 3.265,
     'norm_ffn': 14.33,
     'norm_final': 195.148,
     'gnorm_a': 26.047,
     'qnorm_c': 200.0,
     'kvnorm_c': 102.229,
     'cache_b_k': 4.66,
     'cache_b_v': 4.793,
     'cache_b_kidx': 4.93,
     'rel_bias': 3.195}
    for name, (base, spread) in spreads.items():
        noise = np.random.default_rng([zlib.crc32(name.encode()), seed]).standard_normal(out[name].shape)
        drawn = base * np.exp(spread * noise) if base else spread * noise
        out[name] = jnp.asarray(drawn.astype(out[name].dtype))
    for name, factor in factors.items():
        out[name] = (out[name] * factor).astype(out[name].dtype)
    return out
```

```python
import math
from contextlib import ExitStack

import numpy as np

import concourse.bass as bass
from concourse import mybir

F32 = mybir.dt.float32
F32R = mybir.dt.float32r
BF16 = mybir.dt.bfloat16
I32 = mybir.dt.int32
U8 = mybir.dt.uint8
ALU = mybir.AluOpType
ACT = mybir.ActivationFunctionType
AXX = mybir.AxisListType.X

P = 128
D = 1024
KT = D // P
SEQ = 512
META = 16
LP = SEQ + META
NS = 8
TOK = LP + NS
HALF = TOK // 2
NT = 5
H = 8
DH = 64
QKV = 3 * H * DH
PAST = 4096
PAGE = 128
NPAGES = PAST // PAGE
TOPK_P = 128
TOPK_S = 256
KV = 256
QL = 384
ROPE = 32
VC = 128
DFF = 4096
EPS = 1e-6
NEG = -1e30
FAR = -3.0e38
TAKEN = -3.3e38
PICKED = -3.2e38
MLA_SCALE = float((64 + 32) ** -0.5)
C_Q, C_ALPHA, C_BETA, C_GATE = 0, 1536, 1544, 1552
C_QB, C_KB, C_VB, C_QI, C_WI, C_KI = 2064, 2576, 3088, 3600, 4112, 4120
BAND = 784
NRAW = 8
NSPLIT = 2


def rows_of(t):
    return P if t < NT - 1 else META


def constants():
    i = np.arange(P)
    f = np.float32
    c = {}
    c["ident"] = np.eye(P, dtype=f)
    c["ones"] = np.ones((P, P), f)
    c["blk"] = (i[:, None] // 64 == i[None, :] // 64).astype(f)
    c["tri"] = np.where(i[None, :] > i[:, None], f(NEG), f(0)).astype(f)
    c["trifar"] = np.where(i[None, :] > i[:, None], f(FAR), f(0)).astype(f)
    c["incl"] = (i[None, :] >= i[:, None]).astype(f)
    c["strict"] = (i[None, :] > i[:, None]).astype(f)
    c["i64"] = (i[:, None] % 64 == np.arange(64)[None, :]).astype(f)
    c["even"] = (i[:, None] == i[None, :] % 64).astype(f)
    c["odd"] = (i[:, None] == 64 + i[None, :] % 64).astype(f)
    swap = (i // 32) * 32 + (i % 32 + 16) % 32
    c["swap"] = (i[:, None] == swap[None, :]).astype(f)
    sel = np.zeros((P, 12, P), f)
    for h in range(8):
        sel[h, h, :] = 1
    for hp in range(4):
        sel[2 * hp, 8 + hp, :64] = 1
        sel[2 * hp + 1, 8 + hp, 64:] = 1
    c["sel"] = sel.reshape(P, -1)
    inv = (f(10000.0) ** (-np.arange(16, dtype=f) / f(16))).astype(f)
    pos = np.concatenate([np.arange(LP), np.full(NS, PAST)]).astype(f)
    ang = (pos[:, None] * inv[None, :]).astype(f)
    cos, sin = np.cos(ang).astype(f), np.sin(ang).astype(f)
    r = i % 32
    c["cos"] = cos[:, r % 16].T.copy()
    c["sin"] = (np.where(r < 16, -1, 1)[:, None] * sin[:, r % 16].T).astype(f)
    lv = np.zeros((14, P, P), f)
    for l in range(7):
        b = 1 << l
        m = (i[:, None] // (2 * b) == i[None, :] // (2 * b)) & (i[:, None] % (2 * b) >= b) & (i[None, :] % (2 * b) < b)
        lv[l] = m
        lv[7 + l] = m.T
    masks = lv.transpose(1, 0, 2).reshape(P, -1).copy()
    dist = BAND - 129 - np.arange(BAND)
    oh = np.where(dist >= 0, bucket(np.maximum(dist, 0))[None, :] == np.arange(32)[:, None], 0).astype(f)
    return c, masks, oh


def bucket(dist):
    f = np.float32
    ratio = np.log(np.maximum(dist, 1).astype(f) / f(16)) / f(math.log(64))
    large = 16 + (ratio * f(16)).astype(np.int32)
    return np.where(dist < 16, dist, np.minimum(large, 31))


CONST_COLS = [("ident", 128), ("ones", 128), ("blk", 128), ("tri", 128), ("trifar", 128), ("incl", 128),
              ("strict", 128), ("i64", 64), ("even", 128), ("odd", 128), ("swap", 128), ("sel", 1536)]


def sample_constants():
    i = np.arange(P)
    f = np.float32
    c = {}
    c["pcol"] = np.stack([i % 32, 4 * i], 1).astype(f)
    hsel = np.zeros((P, P), f)
    for h in range(8):
        hsel[64 + h, [32 * j + h for j in range(4)]] = 1
    c["hsel"] = hsel
    c["bm4"] = (i[:, None] // 32 == np.arange(4)[None, :]).astype(f)
    c["iota16"] = np.broadcast_to(np.arange(16), (P, 16)).astype(f)
    first = [int(np.argmax(bucket(np.arange(PAST + 1)) >= j)) for j in range(32)]
    c["thr"] = np.broadcast_to(np.array(first), (P, 32)).astype(f)
    b, h = i[:, None] // 8, i[:, None] % 8
    c["e64"] = (i[:, None] == np.arange(64)[None, :] // 8).astype(f)
    c["hm8"] = (h == np.arange(8)[None, :]).astype(f)
    m = np.arange(32)[None, :]
    c["maskA"] = ((b == m % 8) & (h // 2 == m // 8)).astype(f)
    c["parsel"] = (h % 2 == i[None, :] // 64).astype(f)
    c["hmask"] = ((i[:, None] % 32) == np.arange(8)[None, :]).astype(f)
    c["gres"] = np.broadcast_to(np.arange(64) % 8 != 0, (P, 64)).astype(f)
    s = np.tile(np.arange(4), 64)[None, :]
    g = np.tile(np.repeat(np.arange(8), 4), 8)[None, :]
    c["kpos"] = (512 * g + 4 * i[:, None] + s).astype(f)
    return c


SAMPLE_COLS = [("pcol", 2), ("hsel", 128), ("bm4", 4), ("iota16", 16), ("thr", 32), ("e64", 64), ("hm8", 8),
               ("maskA", 32), ("parsel", 128), ("hmask", 8), ("gres", 64), ("kpos", 256)]


def more_constants():
    c = sample_constants()
    return {"dconst": np.concatenate([c[n] for n, _ in SAMPLE_COLS], 1).astype(np.float32)}


ROPE_COLS = [("cos", TOK), ("sin", TOK), ("bsel", 256), ("rep", 512)]


def rope_constants():
    c = constants()[0]
    i, m = np.arange(P)[:, None], np.arange(P)[None, :]
    c["bsel"] = np.concatenate([i == META + 4 * bg + m // 32 for bg in range(2)], 1)
    c["rep"] = np.concatenate([i == ROPE * r + m % ROPE for r in range(4)], 1)
    return {"rope": np.concatenate([c[n] for n, _ in ROPE_COLS], 1).astype(np.float32)}


class Chain:

    def __init__(self, sem):
        self.sem, self.n = sem, 0

    def link(self, eng, ins):
        self.n += 1
        ins.then_inc(self.sem, 1)
        eng.wait_ge(self.sem, self.n)


def trunk(nc, d, out):
    ctx = ExitStack()
    with ctx:
        def sem(name):
            return ctx.enter_context(nc.semaphore(name))

        uses = {}

        def sb(name, shape, dt=F32, scope=ctx):
            uses[name] = uses.get(name, 0) + 1
            name += str(uses[name]) if uses[name] > 1 else ""
            return scope.enter_context(nc.sbuf_tensor(name, shape, dt))

        consts = sb("consts", [P, sum(n for _, n in CONST_COLS)])
        cst, at = {}, 0
        for name, n in CONST_COLS:
            cst[name] = consts[:, at:at + n]
            at += n
        sel_h = cst["sel"].rearrange("p (s m) -> p s m", s=12)
        level_masks = sb("level_masks", [P, 14, P], U8)
        vec = sb("vec", [P, 128])
        hT = sb("hT", [P, KT, TOK])
        raw = sb("raw", [P, NRAW, KT, P])
        w_hi = sb("w_hi", [P, NSPLIT, KT, P], F32R)
        w_lo = sb("w_lo", [P, NSPLIT, KT, P], F32R)
        page_idx = sb("page_idx", [P, NS * NPAGES // 4], I32)
        oT = sb("oT", [P, KT, TOK])
        PS = [ctx.enter_context(nc.psum_tensor(f"ps{i}", [P, 1024], F32)) for i in range(4)]
        NORM1, FFN1, NORM2, FFN2, FINAL, QN, KN, CONVW, GN, AEXP, DTB, EPSC, SPARE = (
            0, 8, 16, 24, 32, 40, 43, 45, 93, 94, 95, 96, 97)

        const_in = sem("const_in")
        out_done = sem("out_done")
        raw_in = [sem(f"raw_in{i}") for i in range(NRAW)]
        hi_done = sem("hi_done")
        split_done = sem("split_done")
        gemm_done = sem("gemm_done")
        psum_free = [sem("psum_free0"), sem("psum_free1")]
        sq_ready, sq_used = sem("sq_ready"), sem("sq_used")
        std_ready, rstd_ready = sem("std_ready"), sem("rstd_ready")
        normed, hi_ready, lo_ready = sem("normed"), sem("hi_ready"), sem("lo_ready")
        chain_act, chain_dve, chain_pool = Chain(sem("chain_act")), Chain(sem("chain_dve")), Chain(sem("chain_pool"))
        outs = [0]

        def store(eng, dst, src):
            outs[0] += 1
            eng.dma_start(dst, src).then_inc(out_done, 16)

        jobs, raw_count, raw_total = [], [], [0] * NRAW

        def add_job(parts, nk=KT):
            n = len(jobs)
            jobs.append((parts, nk))
            raw_total[n % NRAW] += 16 * len(parts)
            raw_count.append(raw_total[n % NRAW])
            return n

        def blocks(w, c0, c1):
            v = w.rearrange("(k p) c -> p k c", p=P)
            return [add_job([(0, v[:, :, c:c + P])]) for c in range(c0, c1, P)]

        loaded = [0]

        def load_job(eng, n, src=None, i=0, per=0):
            parts, nk = jobs[n]
            if n >= NRAW:
                eng.wait_ge(split_done, i * per + (n - NRAW + 1))
            for c, s in ([(0, src)] if src is not None else parts):
                eng.dma_start(raw[:, n % NRAW, :nk, c:c + s.shape[-1]], s).then_inc(raw_in[n % NRAW], 16)

        def load_weights(eng, upto):
            for n in range(loaded[0], min(upto, len(jobs))):
                load_job(eng, n)
            loaded[0] = max(loaded[0], min(upto, len(jobs)))

        def split_high(act, n, i=0, per=0):
            nk = jobs[n][1]
            act.wait_ge(raw_in[n % NRAW], i * (per // NRAW * 16) + raw_count[n])
            if n >= NSPLIT:
                act.wait_ge(gemm_done, i * per + (n - NSPLIT + 1))
            nc.scalar.activation(w_hi[:, n % NSPLIT, :nk], raw[:, n % NRAW, :nk], ACT.Copy).then_inc(hi_done, 1)

        def split_low(dve, n, i=0, per=0):
            nk = jobs[n][1]
            dve.wait_ge(hi_done, i * per + (n + 1))
            nc.vector.tensor_tensor(w_lo[:, n % NSPLIT, :nk], raw[:, n % NRAW, :nk],
                                    w_hi[:, n % NSPLIT, :nk].bitcast(F32), ALU.subtract).then_inc(split_done, 1)

        def halves(ap):
            return ap.rearrange("p (a n) -> p a n", a=2)

        def job_psum(n):
            return halves(PS[n % 2][:, :])[:, :, :HALF]

        def multiply(pe, n, x_hi, x_lo, before_k=None, i=0, per=0):
            nk = jobs[n][1]
            pe.wait_ge(split_done, i * per + (n + 1))
            if n >= 2:
                pe.wait_ge(psum_free[n % 2], i * (per // 2) + n // 2)
            for k in range(nk):
                if before_k:
                    before_k(k)
                hi, lo = w_hi[:, n % NSPLIT, k], w_lo[:, n % NSPLIT, k]
                for w, x, a, b in ((hi, x_hi, k == 0, False), (hi, x_lo, False, False), (lo, x_hi, False, k == nk - 1)):
                    for s in range(2):
                        mm = nc.tensor.matmul(PS[n % 2][:, 512 * s:512 * s + HALF], w, x[:, k, s * HALF:(s + 1) * HALF],
                                              start=a, stop=b)
            mm.then_inc(gemm_done, 1)

        def add_to_residual(dve, n, m, i=0, per=0):
            dve.wait_ge(gemm_done, i * per + (n + 1))
            nc.vector.tensor_tensor(halves(hT[:, m]), halves(hT[:, m]), job_psum(n), ALU.add).then_inc(psum_free[n % 2], 1)

        count = {"sq": 0, "norm": 0, "tile": 0, "normed": 0}

        def split(src, nk, hi, lo, before=None):
            t0 = count["tile"]
            count["tile"] += nk

            def on_act(act):
                for k in range(nk):
                    nc.scalar.activation(hi[:, k], src[:, k], ACT.Copy).then_inc(hi_ready, 1)

            def on_dve(dve):
                for k in range(nk):
                    dve.wait_ge(hi_ready, t0 + k + 1)
                    nc.vector.tensor_tensor(lo[:, k], src[:, k], hi[:, k].bitcast(F32), ALU.subtract).then_inc(lo_ready, 1)

            return on_act, on_dve

        def norm(src, nk, width, wcol, hi, lo, keep=None, before=None):
            sq0, n0, t0 = count["sq"], count["norm"], count["tile"]
            count["sq"] += nk
            count["norm"] += 1
            e0 = count["normed"]
            count["normed"] += nk
            if hi is not None:
                count["tile"] += nk
            sqb, tmp, rstd = oT[:, 0:2], oT[:, 2:4], oT[:, 4]
            dst = (lambda k: keep[:, k]) if keep is not None else (lambda k: tmp[:, k % 2])

            def on_act(act):
                for k in range(nk):
                    if k >= 2:
                        act.wait_ge(sq_used, sq0 + k - 1)
                    if before:
                        before(act, k)
                    nc.scalar.activation(sqb[:, k % 2], src[:, k], ACT.Square).then_inc(sq_ready, 1)
                act.wait_ge(sq_used, sq0 + nk)
                if e0:
                    act.wait_ge(normed, e0)
                nc.scalar.activation(halves(rstd), halves(PS[2][:, :])[:, :, :HALF], ACT.Sqrt,
                                     bias=vec[:, EPSC:EPSC + 1], scale=1.0 / width).then_inc(std_ready, 1)
                if hi is not None:
                    for k in range(nk):
                        act.wait_ge(normed, e0 + k + 1)
                        nc.scalar.activation(hi[:, k], dst(k), ACT.Copy).then_inc(hi_ready, 1)

            def on_pe(pe):
                if n0:
                    pe.wait_ge(std_ready, n0)
                for k in range(nk):
                    pe.wait_ge(sq_ready, sq0 + k + 1)
                    for s in range(2):
                        mm = nc.tensor.matmul(PS[2][:, 512 * s:512 * s + HALF], cst["ones"],
                                              sqb[:, k % 2, s * HALF:(s + 1) * HALF], start=k == 0, stop=k == nk - 1)
                    mm.then_inc(sq_used, 1)

            def on_dve(dve):
                dve.wait_ge(std_ready, n0 + 1)
                nc.vector.reciprocal(rstd, rstd).then_inc(rstd_ready, 1)
                dve.wait_ge(rstd_ready, n0 + 1)

                def lower(k):
                    dve.wait_ge(hi_ready, t0 + k + 1)
                    nc.vector.tensor_tensor(lo[:, k], dst(k), hi[:, k].bitcast(F32), ALU.subtract).then_inc(lo_ready, 1)

                for k in range(nk):
                    if keep is None and k >= 2:
                        dve.wait_ge(lo_ready, t0 + k - 1)
                    nc.vector.scalar_tensor_tensor(dst(k), src[:, k], vec[:, wcol + k:wcol + k + 1], rstd,
                                                   ALU.mult, ALU.mult).then_inc(normed, 1)
                    if hi is not None and k >= 1:
                        lower(k - 1)
                if hi is not None:
                    lower(nk - 1)
                else:
                    dve.wait_ge(normed, e0 + nk)

            return on_act, on_pe, on_dve

        x_in, xt_ready, x_out = sem("x_in"), sem("xt_ready"), sem("x_out")
        N_CONST = 16
        with ExitStack() as scope:
            xrow = sb("xrow", [P, NT, D], scope=scope)
            vrow = sb("vrow", [P, P], scope=scope)
            mrow = sb("mrow", [P, 14 * P], scope=scope)
            with nc.Block() as block:
                @block.sync
                def _(sp):
                    xp, meta, xs = d["x_prompt"][0], d["meta_tokens"], d["x_sample"][:, 0, :]
                    sp.dma_start(consts[:, :], d["consts"]).then_inc(const_in, 16)
                    sp.dma_start(xrow[0:META, 0, :], meta).then_inc(x_in, 16)
                    sp.dma_start(xrow[META:P, 0, :], xp[0:P - META]).then_inc(x_in, 16)
                    sp.dma_start(xrow[:, 1:4, :], xp[P - META:4 * P - META].rearrange("(t p) n -> p t n", p=P)).then_inc(x_in, 16)
                    sp.dma_start(xrow[0:META, 4, :], xp[4 * P - META:]).then_inc(x_in, 16)
                    sp.dma_start(xrow[META:META + NS, 4, :], xs).then_inc(x_in, 16)
                    load_weights(sp, NRAW)

                @block.scalar
                def _(act):
                    rows = [(d["norm_mix"][0], 8), (d["norm_ffn"][0], 8), (d["norm_mix"][1], 8), (d["norm_ffn"][1], 8),
                            (d["norm_final"], 8), (d["qnorm_c"][0], 3), (d["kvnorm_c"][0], 2)]
                    r = 0
                    for v, n in rows:
                        act.dma_start(vrow[r:r + n, :], v.rearrange("(k p) -> k p", p=P)).then_inc(const_in, 16)
                        r += n
                    for j in range(4):
                        act.dma_start(vrow[r:r + 12, :], d["conv_a"][0, j].rearrange("(k p) -> k p", p=P)).then_inc(const_in, 16)
                        r += 12
                    act.dma_start(mrow[:, :], d["masks"]).then_inc(const_in, 16)
                    with nc.allow_non_contiguous_dma(reason="a few short vectors onto partitions"):
                        act.dma_start(vec[0:H, AEXP:AEXP + 1], d["a_log"].rearrange("o h -> h o")).then_inc(const_in, 16)
                        act.dma_start(vec[0:H, DTB:DTB + 1], d["dt_bias_a"].rearrange("o h -> h o")).then_inc(const_in, 16)
                        act.dma_start(vec[0:DH, GN:GN + 1], d["gnorm_a"].rearrange("o h -> h o")).then_inc(const_in, 16)
                        act.dma_start(vec[DH:P, GN:GN + 1], d["gnorm_a"].rearrange("o h -> h o")).then_inc(const_in, 16)
                    for k in range(KT):
                        act.wait_ge(xt_ready, k + 1)
                        nc.scalar.activation(hT[:, k], PS[k % 2][:, :TOK], ACT.Copy).then_inc(x_out, 1)
                    act.wait_ge(xt_ready, KT + 1)
                    nc.scalar.activation(vec[:, 0:93], PS[2][:, 0:93], ACT.Copy).then_inc(x_out, 1)

                @block.vector
                def _(dve):
                    nc.vector.memset(vec[:, EPSC:EPSC + 1], EPS).then_inc(chain_dve.sem, 1)
                    chain_dve.n += 1
                    dve.wait_ge(const_in, 16 * N_CONST + 16)
                    link = chain_dve.link
                    link(dve, nc.vector.tensor_copy(level_masks[:, :, :].rearrange("p l m -> p (l m)"), mrow[:, :]))

                @block.tensor
                def _(pe):
                    pe.wait_ge(const_in, 16 * N_CONST + 16)
                    pe.wait_ge(x_in, 16 * 5)
                    for k in range(KT):
                        if k >= 2:
                            pe.wait_ge(x_out, k - 1)
                        for t in range(NT):
                            n = P if t < 4 else META + NS
                            mm = nc.tensor.transpose(PS[k % 2][:, t * P:t * P + n], xrow[:n, t, k * P:(k + 1) * P],
                                                     cst["ident"][:n, :n])
                        mm.then_inc(xt_ready, 1)
                    nc.tensor.transpose(PS[2][:, 0:93], vrow[0:93, :], cst["ident"][:93, :93]).then_inc(xt_ready, 1)

        L0 = ctx.enter_context(ExitStack())
        qbT, kbT = sb("qbT", [P, 4, TOK], scope=L0), sb("kbT", [P, 4, TOK], scope=L0)
        vbT, qiT = sb("vbT", [P, 4, TOK], scope=L0), sb("qiT", [P, 4, TOK], scope=L0)
        abT, kiT = sb("abT", [P, TOK], scope=L0), sb("kiT", [P, TOK], scope=L0)
        G0 = L0.enter_context(ExitStack())
        qkvT, gateT = sb("qkvT", [P, 12, TOK], scope=G0), sb("gateT", [P, 4, TOK], scope=G0)
        w_in = d["w_in_ab"][0]
        w_in_v = w_in.rearrange("(k p) c -> p k c", p=P)
        JQKV = blocks(w_in, C_Q, C_ALPHA)
        JAB = add_job([(0, w_in_v[:, :, C_ALPHA:C_ALPHA + H]), (32, w_in_v[:, :, C_BETA:C_BETA + H]),
                       (64, w_in_v[:, :, C_WI:C_WI + H])])
        JGATE = blocks(w_in, C_GATE, C_QB)
        JKI = add_job([(0, w_in_v[:, :, C_KI:C_KI + DH]), (DH, w_in_v[:, :, C_KI:C_KI + DH])])
        JQI, JQB, JKB, JVB = (blocks(w_in, c, c + H * DH) for c in (C_QI, C_QB, C_KB, C_VB))
        J0 = list(range(len(jobs)))
        JO = blocks(d["w_out_ab"][0], 0, D)

        def project_to(n):
            if n < JAB:
                return None
            if n == JAB:
                return abT[:, :]
            if n == JKI:
                return kiT[:, :]
            for dst, js in ((gateT, JGATE), (qiT, JQI), (qbT, JQB), (kbT, JKB), (vbT, JVB)):
                if n in js:
                    return dst[:, js.index(n)]

        conv_done, conv_out, conv_in, conv_T, conv_Tout = (
            sem(n) for n in ("conv_done", "conv_out", "conv_in", "conv_T", "conv_Tout"))
        silu_done = sem("silu_done")
        with ExitStack() as scope:
            hn_hi, hn_lo = sb("hn_hi", [P, KT, TOK], F32R, scope), sb("hn_lo", [P, KT, TOK], F32R, scope)
            xr = sb("xr", [P, 2, 3 + TOK], scope=scope)
            dec_in = sb("dec_in", [P, 12, NS, 4], scope=scope)
            dec_acc = sb("dec_acc", [P, 12, NS], scope=scope)
            tail = sb("tail", [P, 12, 3 + NS], scope=scope)
            srow = oT[:, 5:8].rearrange("p k n -> p (k n)")[0:3 * NS, :QKV]
            n_act, n_pe, n_dve = norm(hT, KT, D, NORM1, hn_hi, hn_lo)
            with nc.Block() as block:
                @block.sync
                def _(sp):
                    sp.dma_start(srow[:, :], d["state_a_conv"][0].rearrange("b j c -> (b j) c")).then_inc(conv_in, 16)
                    for j in range(2):
                        store(sp, out["a_conv_s"][0, :, j, :], d["state_a_conv"][0, :, j + 1, :])
                    load_weights(sp, len(J0) + NRAW)
                    sp.wait_ge(conv_Tout, 2)

                @block.scalar
                def _(act):
                    n_act(act)
                    split_high(act, 0)
                    for n in J0:
                        if n + 1 < len(J0):
                            split_high(act, n + 1)
                        act.wait_ge(gemm_done, n + 1)
                        if n < JAB:
                            if n >= 2:
                                act.wait_ge(conv_done, 4 * (n - 1))
                                act.wait_ge(conv_out, 2 * (n - 1))
                            nc.scalar.activation(halves(xr[:, n % 2, 3:]), job_psum(n), ACT.Copy)\
                                .then_inc(psum_free[n % 2], 1)
                            act.wait_ge(psum_free[n % 2], n // 2 + 1)
                            nc.scalar.activation(tail[:, n], xr[:, n % 2, LP:], ACT.Copy).then_inc(conv_out, 1)
                            nc.scalar.activation(dec_in[:, n, :, 3], xr[:, n % 2, 3 + LP:], ACT.Copy).then_inc(conv_out, 1)
                            if n >= 1:
                                act.wait_ge(conv_done, 4 * n)
                                nc.scalar.activation(qkvT[:, n - 1, :LP], qkvT[:, n - 1, :LP], ACT.Silu).then_inc(silu_done, 1)
                        else:
                            if n == JAB:
                                act.wait_ge(conv_done, 4 * n)
                                nc.scalar.activation(qkvT[:, n - 1, :LP], qkvT[:, n - 1, :LP], ACT.Silu).then_inc(silu_done, 1)
                            nc.scalar.activation(halves(project_to(n)), job_psum(n), ACT.Copy).then_inc(psum_free[n % 2], 1)
                    act.wait_ge(conv_T, 1)
                    nc.scalar.activation(dec_in[:, :, :, 0:3],
                                         PS[3][:, 0:288].rearrange("p (m b j) -> p m b j", m=12, b=NS), ACT.Copy).then_inc(conv_out, 1)
                    act.wait_ge(conv_done, 4 * 12 + 1)
                    nc.scalar.activation(qkvT[:, :, LP:], dec_acc[:, :, :], ACT.Silu).then_inc(silu_done, 1)
                    act.wait_ge(conv_T, 2)
                    act.wait_ge(conv_out, 2 * 12 + 1)
                    for c in range(2):
                        w = 1024 if c == 0 else 512
                        nc.scalar.activation(srow[0:3 + NS, c * 1024:c * 1024 + w], PS[2 + c][0:3 + NS, :w],
                                             ACT.Copy).then_inc(conv_Tout, 1)
                    act.wait_ge(conv_Tout, 2)
                    store(act, out["a_conv_p"][0, 0], srow[0:3, :])
                    store(act, out["a_conv_s"][0, :, 2, :], srow[3:3 + NS, :])
                    act.wait_ge(out_done, 16 * outs[0])

                @block.vector
                def _(dve):
                    chain_dve.link(dve, nc.vector.memset(xr[:, :, 0:3], 0.0))
                    n_dve(dve)
                    split_low(dve, 0)
                    for n in J0:
                        if n + 1 < len(J0):
                            split_low(dve, n + 1)
                        if n < JAB:
                            dve.wait_ge(psum_free[n % 2], n // 2 + 1)
                            for j in range(4):
                                w = vec[:, CONVW + 12 * j + n:CONVW + 12 * j + n + 1]
                                if j == 0:
                                    ins = nc.vector.tensor_scalar(qkvT[:, n, :LP], xr[:, n % 2, 0:LP], w, None, ALU.mult)
                                else:
                                    dve.wait_ge(conv_done, 4 * n + j)
                                    ins = nc.vector.scalar_tensor_tensor(qkvT[:, n, :LP], xr[:, n % 2, j:j + LP], w,
                                                                         qkvT[:, n, :LP], ALU.mult, ALU.add)
                                ins.then_inc(conv_done, 1)
                    dve.wait_ge(conv_out, 2 * 12 + 1)
                    tmp = oT[:, 0, 0:12 * NS].rearrange("p (m b) -> p m b", m=12)
                    for j in range(4):
                        w = vec[:, CONVW + 12 * j:CONVW + 12 * j + 12].unsqueeze(2).to_broadcast([P, 12, NS])
                        dst = dec_acc[:, :, :] if j == 0 else tmp
                        chain_dve.link(dve, nc.vector.tensor_tensor(dst, dec_in[:, :, :, j], w, ALU.mult))
                        if j:
                            ins = nc.vector.tensor_tensor(dec_acc[:, :, :], dec_acc[:, :, :], tmp, ALU.add)
                            if j < 3:
                                chain_dve.link(dve, ins)
                            else:
                                ins.then_inc(conv_done, 1)

                @block.tensor
                def _(pe):
                    n_pe(pe)
                    pe.wait_ge(lo_ready, KT)
                    for n in J0:
                        multiply(pe, n, hn_hi, hn_lo)
                    pe.wait_ge(conv_in, 16)
                    for m in range(12):
                        mm = nc.tensor.transpose(PS[3][:, 24 * m:24 * m + 24], srow[:, m * P:(m + 1) * P], cst["ident"][:24, :24])
                    mm.then_inc(conv_T, 1)
                    pe.wait_ge(conv_out, 2 * 12 + 1)
                    for m in range(12):
                        dst = PS[2 + m // 8][0:3 + NS, (m % 8) * P:(m % 8 + 1) * P]
                        mm = nc.tensor.transpose(dst, tail[:, m], cst["ident"])
                    mm.then_inc(conv_T, 1)

        names = ("g_rows", "g_bc", "g_cols", "g_d", "g_e", "g_kb", "g_kk", "g_nat", "g_t1", "g_t1c", "g_p", "g_x",
                 "g_tok", "g_w", "g_wc", "g_vn", "g_vnc", "g_o", "g_oc", "g_s", "g_tile", "g_l2s", "g_l2p", "g_l2r",
                 "g_l2d", "g_st", "g_dp", "g_dd")
        (g_rows, g_bc, g_cols, g_d, g_e, g_kb, g_kk, g_nat, g_t1, g_t1c, g_p, g_x, g_tok, g_w, g_wc, g_vn, g_vnc,
         g_o, g_oc, g_s, g_tile, g_l2s, g_l2p, g_l2r, g_l2d, g_st, g_dp, g_dd) = (sem(n) for n in names)

        def slot(h):
            return (h % 2) * 4 + h // 2

        def levels(t):
            return 7 if t < NT - 1 else 4

        def steps_before(t):
            return sum(levels(u) for u in range(t))

        with ExitStack() as scope:
            work = sb("work", [P, 6, 8, P], scope=scope)
            NAT, QKT, X, XT, T1, EI = (work[:, i] for i in range(6))
            kb = sb("kb", [P, 4, P], scope=scope)
            qg = sb("qg", [P, 4, P], scope=scope)
            kbg, kdec, vbeta, vnew = (sb(n, [P, 8, DH], scope=scope) for n in ("kbg", "kdec", "vbeta", "vnew"))
            wT = sb("wT", [P, 4, P], scope=scope)
            S = sb("S", [P, 4, DH], scope=scope)
            cols = sb("cols", [P, 28], scope=scope)
            ccol = sb("ccol", [P, 3, 8], scope=scope)
            elast = sb("elast", [P, 4], scope=scope)
            rows = oT[0:8, 4:7]
            head_t1 = oT[0:8, 7]
            head_t2, head_reset = (work[0:8, i].rearrange("p s n -> p (s n)")[:, :TOK] for i in range(2))
            reset = head_reset[:, :LP]
            ea = sb("ea", [8, 1], scope=scope)
            dcol = sb("dcol", [P, 2, 4, NS], scope=scope)

            def bch(ap, n):
                return ap.rearrange("p (a b) -> p b a", b=2).unsqueeze(3).to_broadcast([ap.shape[0], 2, 4, n])

            def sl4(ap, n):
                return ap[:n, :, :n].rearrange("p (b a) n -> p b a n", b=2)

            def ps8(i, n):
                return PS[i][:, :].rearrange("p (s n) -> p s n", s=8)[:n, :, :n]

            with nc.Block() as block:
                @block.scalar
                def _(act):
                    t1, t2 = head_t1, head_t2
                    al = abT[0:8, :]
                    chain_act.link(act, nc.scalar.activation(t1, al, ACT.Abs, bias=vec[0:8, DTB:DTB + 1]))
                    chain_act.link(act, nc.scalar.activation(t1, t1, ACT.Exp, scale=-1.0))
                    nc.scalar.activation(ea[:, :], vec[0:8, AEXP:AEXP + 1], ACT.Exp).then_inc(g_rows, 1)
                    nc.scalar.activation(t1, t1, ACT.Ln, bias=1.0).then_inc(g_rows, 1)
                    nc.scalar.activation(t2, al, ACT.Relu, bias=vec[0:8, DTB:DTB + 1]).then_inc(g_rows, 1)
                    nc.scalar.activation(rows[:, 1], abT[32:40, :], ACT.Sigmoid).then_inc(g_rows, 1)
                    act.wait_ge(g_rows, 6)
                    nc.scalar.activation(rows[:, 2], rows[:, 0], ACT.Exp).then_inc(g_rows, 1)
                    for m in range(8):
                        if m >= 2:
                            act.wait_ge(g_l2p, m - 1)
                        nc.scalar.activation(oT[:, m % 2], qkvT[:, m], ACT.Square).then_inc(g_l2s, 1)
                        act.wait_ge(g_l2p, m + 1)
                        if m >= 2:
                            act.wait_ge(g_l2d, m - 1)
                        nc.scalar.activation(halves(oT[:, 2 + m % 2]), job_psum(m), ACT.Sqrt,
                                             bias=vec[:, EPSC:EPSC + 1]).then_inc(g_l2r, 1)

                    for t in range(NT):
                        n, c0 = rows_of(t), P * t
                        act.wait_ge(g_bc, t + 1)
                        nc.scalar.activation(cols[:, :], PS[1][:, 0:28], ACT.Copy).then_inc(g_cols, 1)
                        act.wait_ge(g_cols, 3 * t + 1)
                        nc.scalar.activation(ccol[:n, 0], cols[:n, 0:8], ACT.Exp).then_inc(g_cols, 1)
                        nc.scalar.activation(elast[:, :], cols[:, 24:28], ACT.Exp).then_inc(g_cols, 1)
                        act.wait_ge(g_d, 2 * t + 1)
                        nc.scalar.activation(EI[:n, :, :n], EI[:n, :, :n], ACT.Exp).then_inc(g_e, 1)
                        act.wait_ge(g_d, 2 * t + 2)
                        nc.scalar.activation(ccol[:n, 2], ccol[:n, 2], ACT.Exp).then_inc(g_e, 1)
                        for l in range(1, levels(t)):
                            for g in range(2):
                                s = 2 * (steps_before(t) + l) + g
                                act.wait_ge(g_t1, s + 1)
                                nc.scalar.activation(T1[:n, 4 * g:4 * g + 4, :n], ps8(0, n)[:, 4 * g:4 * g + 4], ACT.Copy)\
                                    .then_inc(g_t1c, 1)
                        act.wait_ge(g_w, t + 1)
                        nc.scalar.activation(wT[:, :, :n], PS[2][:, 0:512].rearrange("p (a n) -> p a n", a=4)[:, :, :n],
                                             ACT.Copy, scale=-1.0).then_inc(g_wc, 1)
                        act.wait_ge(g_vn, t + 1)
                        nc.scalar.activation(vnew[:n].rearrange("p (b a) v -> p b (a v)", b=2),
                                             halves(PS[3][:, :])[:n, :, 0:256], ACT.Copy).then_inc(g_vnc, 1)
                        act.wait_ge(g_o, t + 1)
                        nc.scalar.activation(oT[:, 0:4, c0:c0 + n],
                                             PS[2][:, 512:1024].rearrange("p (a n) -> p a n", a=4)[:, :, :n], ACT.Copy)\
                            .then_inc(g_oc, 1)

                @block.vector
                def _(dve):
                    link = chain_dve.link
                    link(dve, nc.vector.memset(reset, 1.0))
                    for t in range(NT):
                        link(dve, nc.vector.memset(reset[:, P * t:P * t + 1], 0.0))
                    link(dve, nc.vector.memset(S[:, :, :], 0.0))
                    dve.wait_ge(g_rows, 4)
                    t1, t2 = head_t1, head_t2
                    link(dve, nc.vector.tensor_tensor(t1, t1, t2, ALU.add))
                    nc.vector.tensor_scalar(rows[:, 0], t1, ea[:, 0:1], -1.0, ALU.mult, ALU.mult).then_inc(g_rows, 1)
                    dve.wait_ge(g_rows, 5)
                    nc.vector.tensor_tensor_scan(rows[:, 0, :LP], reset, rows[:, 0, :LP], 0.0, ALU.mult, ALU.add)\
                        .then_inc(g_rows, 1)
                    for m in range(8):
                        dve.wait_ge(g_l2r, m + 1)
                        r = oT[:, 2 + m % 2]
                        link(dve, nc.vector.reciprocal(r, r))
                        nc.vector.scalar_tensor_tensor(qkvT[:, m], qkvT[:, m], 0.125 if m < 4 else 1.0, r,
                                                       ALU.mult, ALU.mult).then_inc(g_l2d, 1)
                    for t in range(NT):
                        n, c0 = rows_of(t), P * t
                        dve.wait_ge(g_cols, 3 * t + 3)
                        link(dve, nc.vector.tensor_tensor(sl4(EI, n), ps8(0, n).rearrange("p (b a) n -> p b a n", b=2),
                                                          bch(cols[:n, 0:8], n), ALU.subtract))
                        nc.vector.tensor_scalar(EI[:n, :, :n], EI[:n, :, :n], 0.0, None, ALU.min).then_inc(g_d, 1)
                        nc.vector.tensor_tensor(ccol[:n, 2], cols[:n, 16:24], cols[:n, 0:8], ALU.subtract).then_inc(g_d, 1)
                        bp = PS[1][:, 512:1024].rearrange("p (a n) -> p a n", a=4)[:, :, :n]
                        ep = PS[2][:, 0:512].rearrange("p (a n) -> p a n", a=4)[:, :, :n]
                        nc.vector.scalar_tensor_tensor(kb[:, :, :n], qkvT[:, 4:8, c0:c0 + n], -1.0, bp,
                                                       ALU.mult, ALU.mult).then_inc(g_kb, 1)
                        nc.vector.tensor_tensor(qg[:, :, :n], qkvT[:, 0:4, c0:c0 + n], ep, ALU.mult).then_inc(g_kb, 1)
                        link(dve, nc.vector.tensor_tensor(ccol[:n, 1], ccol[:n, 0], cols[:n, 8:16], ALU.mult))
                        dve.wait_ge(g_e, 2 * t + 2)
                        ktok = PS[2][:n, 512:1024].rearrange("p (h v) -> p h v", h=8)
                        vtok = PS[3][:n, 0:512].rearrange("p (h v) -> p h v", h=8)

                        def bcv(c):
                            return c.unsqueeze(2).to_broadcast([n, 8, DH])
                        nc.vector.tensor_tensor(kbg[:n], ktok, bcv(ccol[:n, 1]), ALU.mult).then_inc(g_tok, 1)
                        nc.vector.tensor_tensor(kdec[:n], ktok, bcv(ccol[:n, 2]), ALU.mult).then_inc(g_tok, 1)
                        nc.vector.tensor_tensor(vbeta[:n], vtok, bcv(cols[:n, 8:16]), ALU.mult).then_inc(g_tok, 1)
                        link(dve, nc.vector.tensor_tensor(
                            EI[:n, :, :n], EI[:n, :, :n],
                            cst["incl"][:n, :n].unsqueeze(1).to_broadcast([n, 8, n]), ALU.mult))
                        eye = cst["ident"][:n, :n].unsqueeze(1).to_broadcast([n, 8, n])
                        link(dve, nc.vector.tensor_copy(X[:n, :, :n], eye))
                        link(dve, nc.vector.tensor_copy(XT[:n, :, :n], eye))
                        dve.wait_ge(g_kk, 2 * t + 1)
                        link(dve, nc.vector.tensor_tensor(NAT[:n, :, :n], ps8(0, n), EI[:n, :, :n], ALU.mult))
                        dve.wait_ge(g_kk, 2 * t + 2)
                        nc.vector.tensor_tensor(QKT[:n, :, :n], ps8(1, n), EI[:n, :, :n], ALU.mult).then_inc(g_nat, 1)
                        last = levels(t) - 1
                        for l in range(levels(t)):
                            for g in range(2):
                                s = 2 * (steps_before(t) + l) + g
                                hs = slice(4 * g, 4 * g + 4)
                                m, mT = (level_masks[:n, i, :n].unsqueeze(1).to_broadcast([n, 4, n]) for i in (l, 7 + l))
                                if l == 0:
                                    dve.wait_ge(g_t1, s + 1)
                                    link(dve, nc.vector.copy_predicated(XT[:n, hs, :n], mT, NAT[:n, hs, :n]))
                                    ins = nc.vector.copy_predicated(X[:n, hs, :n], m, ps8(0, n)[:, hs])
                                else:
                                    dve.wait_ge(g_p, s + 1 - 2 * (t + 1))
                                    ins = nc.vector.copy_predicated(XT[:n, hs, :n], mT, ps8(3, n)[:, hs])
                                    if l < last:
                                        link(dve, ins)
                                        ins = nc.vector.copy_predicated(X[:n, hs, :n], m, ps8(2, n)[:, hs])
                                ins.then_inc(g_x, 1)
                        dve.wait_ge(g_s, t + 1)
                        link(dve, nc.vector.tensor_tensor(S[:, :, :], S[:, :, :],
                                                          elast[:, :].unsqueeze(2).to_broadcast([P, 4, DH]), ALU.mult))
                        nc.vector.tensor_tensor(S[:, :, :], S[:, :, :],
                                                PS[1][:, 0:256].rearrange("p (a v) -> p a v", a=4), ALU.add).then_inc(g_tile, 1)

                @block.tensor
                def _(pe):
                    for m in range(8):
                        pe.wait_ge(g_l2s, m + 1)
                        if m >= 2:
                            pe.wait_ge(g_l2r, m - 1)
                        for s in range(2):
                            mm = nc.tensor.matmul(PS[m % 2][:, 512 * s:512 * s + HALF], cst["blk"],
                                                  oT[:, m % 2, s * HALF:(s + 1) * HALF], start=True, stop=True)
                        mm.then_inc(g_l2p, 1)
                    pe.wait_ge(g_rows, 7)
                    pe.wait_ge(g_l2d, 8)
                    for t in range(NT):
                        n, c0 = rows_of(t), P * t
                        end = c0 + n
                        if t:
                            pe.wait_ge(g_tile, t)
                            pe.wait_ge(g_oc, t)
                        ident = cst["ident"]
                        for h in range(H):
                            nc.tensor.matmul(PS[0][:n, slot(h) * P:slot(h) * P + n], sel_h[0:8, h, :n], rows[:, 0, c0:end],
                                             start=True, stop=True)
                        nc.tensor.transpose(PS[1][:n, 0:8], rows[:, 0, c0:end], ident[:8, :8])
                        nc.tensor.transpose(PS[1][:n, 8:16], rows[:, 1, c0:end], ident[:8, :8])
                        nc.tensor.matmul(PS[1][:, 16:24], rows[:, 0, end - 1:end].to_broadcast([8, P]), ident[:8, :8],
                                         start=True, stop=True)
                        for a in range(4):
                            nc.tensor.matmul(PS[1][:, 24 + a:25 + a], sel_h[0:8, 8 + a, :], rows[:, 0, end - 1:end],
                                             start=True, stop=True)
                        for a in range(4):
                            nc.tensor.matmul(PS[1][:, 512 + P * a:512 + P * a + n], sel_h[0:8, 8 + a, :], rows[:, 1, c0:end],
                                             start=True, stop=True)
                            nc.tensor.matmul(PS[2][:, P * a:P * a + n], sel_h[0:8, 8 + a, :], rows[:, 2, c0:end],
                                             start=True, stop=True)
                            nc.tensor.transpose(PS[2][:n, 512 + P * a:512 + P * a + P], qkvT[:, 4 + a, c0:end], ident)
                            mm = nc.tensor.transpose(PS[3][:n, P * a:P * a + P], qkvT[:, 8 + a, c0:end], ident)
                        mm.then_inc(g_bc, 1)
                        pe.wait_ge(g_kb, 2 * t + 1)
                        for h in range(H):
                            r = slice(64 * (h % 2), 64 * (h % 2) + 64)
                            mm = nc.tensor.matmul(PS[0][:n, slot(h) * P:slot(h) * P + n], qkvT[r, 4 + h // 2, c0:end],
                                                  kb[r, h // 2, :n], start=True, stop=True)
                        mm.then_inc(g_kk, 1)
                        for h in range(H):
                            r = slice(64 * (h % 2), 64 * (h % 2) + 64)
                            mm = nc.tensor.matmul(PS[1][:n, slot(h) * P:slot(h) * P + n], qkvT[r, 4 + h // 2, c0:end],
                                                  qkvT[r, h // 2, c0:end], start=True, stop=True)
                        mm.then_inc(g_kk, 1)
                        pe.wait_ge(g_nat, t + 1)
                        pe.wait_ge(g_kb, 2 * t + 2)
                        pe.wait_ge(g_tok, 3 * t + 3)
                        for l in range(levels(t)):
                            for g in range(2):
                                s = 2 * (steps_before(t) + l) + g
                                if l:
                                    pe.wait_ge(g_x, s - 1)
                                for q in range(4 * g, 4 * g + 4):
                                    mm = nc.tensor.matmul(PS[0][:n, q * P:q * P + n], NAT[:n, q, :n], X[:n, q, :n],
                                                          start=True, stop=True)
                                mm.then_inc(g_t1, 1)
                            for g in range(2):
                                s = 2 * (steps_before(t) + l) + g
                                if l == 0:
                                    continue
                                pe.wait_ge(g_t1c, s + 1 - 2 * (t + 1))
                                for q in range(4 * g, 4 * g + 4):
                                    if l < levels(t) - 1:
                                        nc.tensor.matmul(PS[2][:n, q * P:q * P + n], XT[:n, q, :n], T1[:n, q, :n],
                                                         start=True, stop=True)
                                    mm = nc.tensor.matmul(PS[3][:n, q * P:q * P + n], T1[:n, q, :n], XT[:n, q, :n],
                                                          start=True, stop=True)
                                mm.then_inc(g_p, 1)
                        pe.wait_ge(g_x, 2 * steps_before(t + 1))
                        for h in range(H):
                            r = slice(64 * (h % 2), 64 * (h % 2) + 64)
                            mm = nc.tensor.matmul(PS[2][r, P * (h // 2):P * (h // 2) + n], kbg[:n, h], XT[:n, slot(h), :n],
                                                  start=True, stop=True)
                        mm.then_inc(g_w, 1)
                        pe.wait_ge(g_wc, t + 1)
                        for h in range(H):
                            r = slice(64 * (h % 2), 64 * (h % 2) + 64)
                            o = PS[3][:n, 512 * (h % 2) + 64 * (h // 2):512 * (h % 2) + 64 * (h // 2) + 64]
                            nc.tensor.matmul(o, XT[:n, slot(h), :n], vbeta[:n, h], start=True, stop=False)
                            mm = nc.tensor.matmul(o, wT[r, h // 2, :n], S[r, h // 2], start=False, stop=True)
                        mm.then_inc(g_vn, 1)
                        pe.wait_ge(g_vnc, t + 1)
                        for h in range(H):
                            r = slice(64 * (h % 2), 64 * (h % 2) + 64)
                            o = PS[2][r, 512 + P * (h // 2):512 + P * (h // 2) + n]
                            nc.tensor.matmul(o, S[r, h // 2], qg[r, h // 2, :n], start=True, stop=False)
                            mm = nc.tensor.matmul(o, vnew[:n, slot(h)], QKT[:n, slot(h), :n], start=False, stop=True)
                        mm.then_inc(g_o, 1)
                        for h in range(H):
                            r = slice(64 * (h % 2), 64 * (h % 2) + 64)
                            mm = nc.tensor.matmul(PS[1][r, 64 * (h // 2):64 * (h // 2) + 64], kdec[:n, h], vnew[:n, slot(h)],
                                                  start=True, stop=True)
                        mm.then_inc(g_s, 1)

            Sd, Dd, Td = (work[:, 2 * i:2 * i + 2].rearrange("p a s n -> p (a s n)").rearrange("p (b m v) -> p b m v", b=NS, m=4)
                          for i in range(3))

            def flat(x, i):
                return x[:, 4 * i:4 * i + 4].rearrange("p b m v -> p (b m v)")

            def col(ap):
                return ap.rearrange("p m b -> p b m").unsqueeze(3).to_broadcast([P, NS, 4, DH])

            i64 = cst["i64"].unsqueeze(1).unsqueeze(1).to_broadcast([P, NS, 4, DH])
            s_out, gn_sq, gn_ps, gn_std, gn_done, gate_done = (
                sem(n) for n in ("s_out", "gn_sq", "gn_ps", "gn_std", "gn_done", "gate_done"))
            with nc.Block() as block:
                @block.sync
                def _(sp):
                    for par in range(2):
                        rp = slice(64 * par, 64 * par + 64)
                        sp.dma_start(Sd[rp].rearrange("k b m v -> k (b m) v"),
                                     d["state_a_ssm"][0].rearrange("b (m r) k v -> r k (b m) v", r=2)[par]).then_inc(g_st, 16)
                        store(sp, out["a_ssm_p"][0, 0].rearrange("(m r) k v -> r k m v", r=2)[par], S[rp])
                    sp.wait_ge(s_out, 1)
                    for par in range(2):
                        rp = slice(64 * par, 64 * par + 64)
                        store(sp, out["a_ssm_s"][0].rearrange("b (m r) k v -> r k (b m) v", r=2)[par],
                              Sd[rp].rearrange("k b m v -> k (b m) v"))
                    sp.wait_ge(out_done, 16 * outs[0])

                @block.tensor
                def _(pe):
                    for a in range(4):
                        for i, r in ((0, 2), (1, 1)):
                            mm = nc.tensor.matmul(PS[3][:, 32 * i + 8 * a:32 * i + 8 * a + 8], sel_h[0:8, 8 + a, :],
                                                  rows[:, r, LP:], start=True, stop=True)
                    mm.then_inc(g_dp, 1)
                    for w, x in enumerate((Dd, Td)):
                        pe.wait_ge(g_dd, w + 2)
                        for i in range(2):
                            for s in range(2):
                                mm = nc.tensor.matmul(PS[i][:, 512 * s:512 * s + 512], cst["blk"],
                                                      flat(x, i)[:, 512 * s:512 * s + 512], start=True, stop=True)
                        mm.then_inc(g_dp, 1)
                    for a in range(4):
                        pe.wait_ge(gn_sq, a + 1)
                        if a == 0:
                            pe.wait_ge(g_dd, 4)
                        if a >= 2:
                            pe.wait_ge(gn_std, a - 1)
                        for s in range(2):
                            mm = nc.tensor.matmul(PS[a % 2][:, 512 * s:512 * s + HALF], cst["blk"],
                                                  oT[:, 4 + a % 2, s * HALF:(s + 1) * HALF], start=True, stop=True)
                        mm.then_inc(gn_ps, 1)

                @block.scalar
                def _(act):
                    act.wait_ge(g_dp, 1)
                    nc.scalar.activation(dcol[:, :, :, :].rearrange("p i m b -> p (i m b)"), PS[3][:, 0:64], ACT.Copy)\
                        .then_inc(g_dd, 1)
                    nc.scalar.activation(gateT[:, :, :], gateT[:, :, :], ACT.Silu).then_inc(gate_done, 1)
                    act.wait_ge(g_dd, 4)
                    for a in range(4):
                        if a >= 2:
                            act.wait_ge(gn_ps, a - 1)
                        nc.scalar.activation(oT[:, 4 + a % 2], oT[:, a], ACT.Square).then_inc(gn_sq, 1)
                        act.wait_ge(gn_ps, a + 1)
                        if a >= 2:
                            act.wait_ge(gn_done, a - 1)
                        nc.scalar.activation(halves(oT[:, 6 + a % 2]), job_psum(a), ACT.Sqrt, scale=1.0 / DH,
                                             bias=vec[:, EPSC:EPSC + 1]).then_inc(gn_std, 1)

                @block.vector
                def _(dve):
                    link, tt = chain_dve.link, nc.vector.tensor_tensor
                    kc, vc, qc = (col(qkvT[:, m:m + 4, LP:]) for m in (4, 8, 0))
                    dve.wait_ge(g_st, 32)
                    dve.wait_ge(g_dd, 1)
                    link(dve, tt(Sd, Sd, col(dcol[:, 0]), ALU.mult))
                    link(dve, tt(Td, Sd, kc, ALU.mult))
                    link(dve, tt(Dd, i64, vc, ALU.mult))
                    tt(Dd, Dd, Td, ALU.subtract).then_inc(g_dd, 1)
                    dve.wait_ge(g_dp, 2)
                    for i in range(2):
                        ps = PS[i][:, :].rearrange("p (b m v) -> p b m v", b=4, m=4)
                        link(dve, tt(Dd[:, 4 * i:4 * i + 4], ps,
                                     dcol[:, 1, :, 4 * i:4 * i + 4].rearrange("p m b -> p b m").unsqueeze(3)
                                     .to_broadcast([P, 4, 4, DH]), ALU.mult))
                    link(dve, tt(Dd, Dd, kc, ALU.mult))
                    tt(Sd, Sd, Dd, ALU.add).then_inc(s_out, 1)
                    dve.wait_ge(s_out, 1)
                    tt(Td, Sd, qc, ALU.mult).then_inc(g_dd, 1)
                    dve.wait_ge(g_dp, 3)
                    for i in range(2):
                        ps = PS[i][:, :].rearrange("p (b m v) -> p b m v", b=4, m=4)
                        link(dve, tt(Dd[:, 4 * i:4 * i + 4], ps, i64[:, 0:4], ALU.mult))
                    nc.vector.tensor_reduce(oT[:, 0:4, LP:].rearrange("p m b -> p b m"), Dd, AXX, ALU.add).then_inc(g_dd, 1)
                    dve.wait_ge(gate_done, 1)
                    for a in range(4):
                        dve.wait_ge(gn_std, a + 1)
                        r = oT[:, 6 + a % 2]
                        link(dve, nc.vector.reciprocal(r, r))
                        link(dve, nc.vector.scalar_tensor_tensor(oT[:, a], oT[:, a], vec[:, GN:GN + 1], r, ALU.mult, ALU.mult))
                        tt(oT[:, a], oT[:, a], gateT[:, a], ALU.mult).then_inc(gn_done, 1)
        G0.close()

        names = ("tk_ps", "tk_out", "tk_bias", "tk_bout", "b_in", "ix_ps", "ix_relu", "ix_acc", "at_qk", "at_l",
                 "at_max", "at_exp", "at_p", "at_pt", "at_ptc", "at_pv", "at_pvc", "bias_stored")
        (tk_ps, tk_out, tk_bias, tk_bout, b_in, ix_ps, ix_relu, ix_acc, at_qk, at_l, at_max, at_exp, at_p,
         at_pt, at_ptc, at_pv, at_pvc, bias_stored) = (sem(n) for n in names)
        bias_dram = nc.dram_tensor("bias_rows", [H, P, BAND], F32, kind="Internal")
        LS = L0.enter_context(ExitStack())
        vtok = sb("vtok", [P, NT, H * DH], scope=LS)
        witok = sb("witok", [P, NT, H], scope=LS)

        def width(t):
            return min(P * (t + 1), LP)

        with ExitStack() as scope:
            ktok, kitok = sb("ktok", [P, NT, H * DH], scope=scope), sb("kitok", [P, NT, DH], scope=scope)
            onehot, rb = sb("onehot", [32, BAND], scope=scope), sb("rb", [32, H], scope=scope)
            brow = sb("brow", [H, BAND], scope=scope)
            with nc.Block() as block:
                @block.sync
                def _(sp):
                    sp.dma_start(onehot[:, :], d["onehot"]).then_inc(b_in, 16)
                    sp.dma_start(rb[:, :], d["rel_bias"]).then_inc(b_in, 16)
                    sp.wait_ge(tk_bout, 2)
                    sp.dma_start(bias_dram.ap(), brow[:, :].unsqueeze(1).to_broadcast([H, P, BAND])).then_inc(bias_stored, 16)
                    sp.wait_ge(tk_out, 4 * NT)
                    for src, name, w in ((ktok, "b_k", 0), (vtok, "b_v", 0), (kitok, "b_kidx", 1)):
                        full, last = src[:, 0:4], src[:META, 4]
                        pr, s = out[name + "_p"][0, 0], out[name + "_s"][0, :, 0]
                        if not w:
                            pr, s = pr.rearrange("t h d -> t (h d)"), s.rearrange("b h d -> b (h d)")
                        store(sp, pr[0:4 * P].rearrange("(t p) n -> p t n", p=P), full)
                        store(sp, pr[4 * P:], last)
                        store(sp, s, src[META:META + NS, 4])
                    sp.wait_ge(out_done, 16 * outs[0])
                    sp.wait_ge(bias_stored, 16)

                @block.tensor
                def _(pe):
                    pe.wait_ge(b_in, 32)
                    for s in range(2):
                        mm = nc.tensor.matmul(PS[3][0:H, 512 * s:512 * s + BAND // 2], rb[:, :],
                                              onehot[:, s * BAND // 2:(s + 1) * BAND // 2], start=True, stop=True)
                    mm.then_inc(tk_bias, 1)
                    for t in range(NT):
                        c, n = P * t, P if t < 4 else META + NS
                        if t:
                            pe.wait_ge(tk_out, 4 * t)
                        for a in range(4):
                            nc.tensor.transpose(PS[0][:n, P * a:P * a + P], kbT[:, a, c:c + n], cst["ident"])
                            nc.tensor.transpose(PS[1][:n, P * a:P * a + P], vbT[:, a, c:c + n], cst["ident"])
                        nc.tensor.transpose(PS[2][:n, 0:DH], kiT[0:DH, c:c + n], cst["ident"][:DH, :DH])
                        nc.tensor.transpose(PS[2][:n, 64:72], abT[64:72, c:c + n], cst["ident"][64:72, 64:72])\
                            .then_inc(tk_ps, 1)

                @block.scalar
                def _(act):
                    act.wait_ge(tk_bias, 1)
                    for s in range(2):
                        nc.scalar.activation(brow[:, s * BAND // 2:(s + 1) * BAND // 2],
                                             PS[3][0:H, 512 * s:512 * s + BAND // 2], ACT.Copy).then_inc(tk_bout, 1)
                    for t in range(NT):
                        n = P if t < 4 else META + NS
                        act.wait_ge(tk_ps, t + 1)
                        nc.scalar.activation(ktok[:n, t], PS[0][:n, 0:512], ACT.Copy).then_inc(tk_out, 1)
                        nc.scalar.activation(vtok[:n, t], PS[1][:n, 0:512], ACT.Copy).then_inc(tk_out, 1)
                        nc.scalar.activation(kitok[:n, t], PS[2][:n, 0:DH], ACT.Copy).then_inc(tk_out, 1)
                        nc.scalar.activation(witok[:n, t], PS[2][:n, 64:72], ACT.Copy, scale=float(H ** -0.5)).then_inc(tk_out, 1)

        pairs = [(h, t) for h in range(H) for t in range(NT)]

        with ExitStack() as scope:
            band = sb("band", [P, H, 640], scope=scope)
            mask = sb("mask", [P, 4, LP], scope=scope)
            relu = sb("relu", [P, 2, LP], scope=scope)
            L, pr = sb("L", [P, 2, LP], scope=scope), sb("pr", [P, 2, LP], scope=scope)
            PT = sb("PT", [P, 2, NT, LP], scope=scope)
            best = sb("best", [P, 8], scope=scope)
            stat = sb("stat", [P, 2, 3], scope=scope)
            band_in = sem("band_in")
            with nc.Block() as block:
                @block.sync
                def _(sp):
                    for h in range(H):
                        src = bass.AP(tensor=bias_dram, offset=h * P * BAND + 143, ap=[[BAND - 1, P], [1, 640]])
                        sp.dma_start(band[:, h], src).then_inc(band_in, 16)

                @block.tensor
                def _(pe):
                    i = 0
                    for t in range(1, NT):
                        n, w = rows_of(t), width(t)
                        for h in range(H):
                            r = slice(64 * (h % 2), 64 * (h % 2) + 64)
                            if i >= 2:
                                pe.wait_ge(ix_relu, i - 1)
                            for a, b in ((0, min(w, 512)), (512, w)):
                                if b > a:
                                    mm = nc.tensor.matmul(PS[i % 2][:n, a:b], qiT[r, h // 2, P * t:P * t + n], kiT[r, a:b],
                                                          start=True, stop=True)
                            mm.then_inc(ix_ps, 1)
                            i += 1

                    def logits(i):
                        h, t = pairs[i]
                        n, w, r = rows_of(t), width(t), slice(64 * (h % 2), 64 * (h % 2) + 64)
                        if i >= 2:
                            pe.wait_ge(at_l, i - 1)
                        for a, b in ((0, min(w, 512)), (512, w)):
                            if b > a:
                                mm = nc.tensor.matmul(PS[i % 2][:n, a:b], qbT[r, h // 2, P * t:P * t + n],
                                                      kbT[r, h // 2, a:b], start=True, stop=True)
                        mm.then_inc(at_qk, 1)

                    pe.wait_ge(ix_relu, 4 * H)
                    logits(0)
                    for i, (h, t) in enumerate(pairs):
                        if i + 1 < len(pairs):
                            logits(i + 1)
                        n = rows_of(t)
                        pe.wait_ge(at_p, i + 1)
                        if i:
                            pe.wait_ge(at_ptc, i)
                        for kt in range(t + 1):
                            m = rows_of(kt)
                            mm = nc.tensor.transpose(PS[2][:m, P * kt:P * kt + n], pr[:n, i % 2, P * kt:P * kt + m],
                                                     cst["ident"][:n, :n])
                        mm.then_inc(at_pt, 1)
                        if t == NT - 1:
                            pe.wait_ge(at_ptc, i + 1)
                            if h:
                                pe.wait_ge(at_pvc, h)
                            r = slice(64 * (h % 2), 64 * (h % 2) + 64)
                            for kt in range(NT):
                                m = rows_of(kt)
                                for bank, a, b in ((0, 0, 256), (512 - 256, 256, LP)):
                                    q0 = max(a, P * kt)
                                    if q0 < b:
                                        mm = nc.tensor.matmul(PS[3][r, bank + q0:bank + b], vtok[:m, kt, h * DH:(h + 1) * DH],
                                                              PT[:m, h % 2, kt, q0:b], start=kt == 0, stop=kt == NT - 1,
                                                              skip_group_check=True)
                            mm.then_inc(at_pv, 1)

                @block.scalar
                def _(act):
                    i = 0
                    for t in range(1, NT):
                        n, w = rows_of(t), width(t)
                        for h in range(H):
                            act.wait_ge(ix_ps, i + 1)
                            if i >= 2:
                                act.wait_ge(ix_acc, i - 1)
                            nc.scalar.activation(relu[:n, i % 2, :w], PS[i % 2][:n, :w], ACT.Relu, scale=0.125)\
                                .then_inc(ix_relu, 1)
                            i += 1

                    def copy_pt(i):
                        h, t = pairs[i]
                        n, c = rows_of(t), P * t
                        act.wait_ge(at_pt, i + 1)
                        if h >= 2:
                            act.wait_ge(at_pv, h - 1)
                        full = min(t + 1, 4)
                        ins = nc.scalar.activation(PT[:, h % 2, 0:full, c:c + n],
                                                   PS[2][:, 0:512].rearrange("p (k n) -> p k n", k=4)[:, :full, :n], ACT.Copy)
                        if t == NT - 1:
                            ins = nc.scalar.activation(PT[:META, h % 2, 4, c:c + n], PS[2][:META, 512:512 + n], ACT.Copy)
                        ins.then_inc(at_ptc, 1)
                        if t == NT - 1 and h:
                            copy_out(h - 1)

                    def copy_out(h):
                        act.wait_ge(at_pv, h + 1)
                        r = slice(64 * (h % 2), 64 * (h % 2) + 64)
                        nc.scalar.activation(oT[r, 4 + h // 2, 0:256], PS[3][r, 0:256], ACT.Copy)
                        nc.scalar.activation(oT[r, 4 + h // 2, 256:LP], PS[3][r, 512:784], ACT.Copy).then_inc(at_pvc, 1)

                    for i, (h, t) in enumerate(pairs):
                        n, w = rows_of(t), width(t)
                        act.wait_ge(at_max, i + 1)
                        nc.scalar.activation(pr[:n, i % 2, :w], L[:n, i % 2, :w], ACT.Exp, bias=stat[:n, i % 2, 0:1],
                                             accum_out=stat[:n, i % 2, 1:2]).then_inc(at_exp, 1)
                        if i:
                            copy_pt(i - 1)
                    copy_pt(len(pairs) - 1)
                    copy_out(H - 1)

                @block.vector
                def _(dve):
                    link = chain_dve.link
                    i = 0
                    for t in range(1, NT):
                        n, w = rows_of(t), width(t)
                        sc = mask[:n, t - 1, :w]
                        for h in range(H):
                            dve.wait_ge(ix_relu, i + 1)
                            wt = witok[:n, t, h:h + 1]
                            if h == 0:
                                ins = nc.vector.tensor_scalar(sc, relu[:n, i % 2, :w], wt, None, ALU.mult)
                            else:
                                dve.wait_ge(ix_acc, i)
                                ins = nc.vector.scalar_tensor_tensor(sc, relu[:n, i % 2, :w], wt, sc, ALU.mult, ALU.add)
                            ins.then_inc(ix_acc, 1)
                            i += 1
                        dve.wait_ge(ix_acc, i)
                        diag = mask[:n, t - 1, P * t:P * t + n]
                        link(dve, nc.vector.tensor_tensor(diag, diag, cst["trifar"][:n, :n], ALU.add))
                        for _ in range(TOPK_P // 8):
                            link(dve, nc.vector.max(best[:n], sc))
                            link(dve, nc.vector.match_replace(sc, best[:n], sc, TAKEN))
                        link(dve, nc.vector.tensor_scalar(sc, sc, PICKED, NEG, ALU.is_gt, ALU.mult))
                    dve.wait_ge(band_in, 16 * H)

                    def normalise(i):
                        h, t = pairs[i]
                        n, w = rows_of(t), width(t)
                        dve.wait_ge(at_exp, i + 1)
                        link(dve, nc.vector.reciprocal(stat[:n, i % 2, 2:3], stat[:n, i % 2, 1:2]))
                        nc.vector.tensor_scalar(pr[:n, i % 2, :w], pr[:n, i % 2, :w], stat[:n, i % 2, 2:3], None, ALU.mult)\
                            .then_inc(at_p, 1)

                    for i, (h, t) in enumerate(pairs):
                        n, w = rows_of(t), width(t)
                        dve.wait_ge(at_qk, i + 1)
                        if i >= 2:
                            dve.wait_ge(at_exp, i - 1)
                            dve.wait_ge(at_pt, i - 1)
                        l = L[:n, i % 2, :w]
                        y = 512 - P * t
                        nc.vector.scalar_tensor_tensor(l, PS[i % 2][:n, :w], 0.125, band[:n, h, y:y + w],
                                                       ALU.mult, ALU.add).then_inc(at_l, 1)
                        dve.wait_ge(at_l, i + 1)
                        m = mask[:n, t - 1, :w] if t else cst["tri"]
                        link(dve, nc.vector.tensor_tensor(l, l, m, ALU.add))
                        nc.vector.tensor_reduce(stat[:n, i % 2, 0:1], l, AXX, ALU.max, negate=True).then_inc(at_max, 1)
                        if i:
                            normalise(i - 1)
                    normalise(len(pairs) - 1)
        LS.close()

        names = ("pt_in", "pg_idx", "kx_ps", "kx_T", "kx_sc", "kx_relu", "kx_sum", "kx_got", "dq_ps", "dq_got",
                 "sl_out", "sl_back", "dx_pe", "dx_act", "dx_dve", "k_used", "dc_in", "z_set")
        (pt_in, pg_idx, kx_ps, kx_T, kx_sc, kx_relu, kx_sum, kx_got, dq_ps, dq_got,
         sl_out, sl_back, dx_pe, dx_act, dx_dve, k_used, dc_in, z_set) = (sem(n) for n in names)
        NKX = 8
        kx_sem = [sem(f"kx_in{i}") for i in range(NKX)]
        G = PAST // (4 * P)
        NC = NS * G * 4
        slots_dram = nc.dram_tensor("slot_rows", [2, NS, TOPK_S], F32, kind="Internal")
        LD = L0.enter_context(ExitStack())
        dconst = sb("dconst", [P, sum(n for _, n in SAMPLE_COLS)], scope=LD)
        dc, at = {}, 0
        for name, n in SAMPLE_COLS:
            dc[name] = dconst[:, at:at + n]
            at += n
        pages = sb("pages", [P, NS * NPAGES], I32, scope=LD)
        pagef = sb("pagef", [P, NS * G], scope=LD)
        SC = sb("SC", [P, NS, 33], scope=LD)
        wsel = sb("wsel", [P, 2, 4], scope=LD)
        qix = sb("qix", [P, NS, H], scope=LD)
        selnew = sb("selnew", [P, NS], scope=LD)
        ridx = sb("ridx", [P, 2, NS], I32, scope=LD)
        posf = sb("posf", [P, 2, NS], scope=LD)
        with ExitStack() as scope:
            kx = sb("kx", [P, NKX, 256], scope=scope)
            kxT = sb("kxT", [P, 2, 4, 512], scope=scope)
            rx = sb("rx", [P, 2, 1024], scope=scope)
            rn = sb("rn", [P, 2], scope=scope)
            with nc.Block() as block:
                @block.sync
                def _(sp):
                    sp.dma_start(dconst[:, :], d["dconst"]).then_inc(dc_in, 16)
                    sp.dma_start(pages[:, :], d["page_table"].rearrange("b n -> (b n)").partition_broadcast(P)).then_inc(pt_in, 16)

                @block.gpsimd
                def _(pool):
                    pool.wait_ge(pg_idx, 6)
                    src = d["cache_b_kidx"][0].rearrange("n (r s) e -> (n r) (s e)", s=4)
                    for i in range(NS * G):
                        it, j, g2 = i // 8, (i // 2) % 4, i % 2
                        b, g = 4 * (it // 4) + j, 2 * (it % 4) + g2
                        if i >= NKX:
                            pool.wait_ge(kx_ps, 4 * (it - 1) + j + 1)
                        pool.indirect_dma_start(kx[:, i % NKX], None, src,
                                                bass.IndirectOffsetOnAxis(ap=page_idx[:, G * b + g:G * b + g + 1], axis=0))\
                            .then_inc(kx_sem[i % NKX], 16)

                @block.vector
                def _(dve):
                    link = chain_dve.link
                    dve.wait_ge(dc_in, 16)
                    dve.wait_ge(pt_in, 16)
                    nc.vector.memset(SC[:, :, 32:33], FAR).then_inc(z_set, 1)
                    pv = pages[:, :].rearrange("p (c q) -> p c q", q=4)
                    for q in range(4):
                        r = slice(32 * q, 32 * q + 32)
                        nc.vector.tensor_copy(pagef[r, :], pv[r, :, q]).then_inc(pg_idx, 1)
                    dve.wait_ge(pg_idx, 4)
                    nc.vector.tensor_scalar(pagef[:, :], pagef[:, :], 32.0, dc["pcol"][:, 0:1], ALU.mult, ALU.add)\
                        .then_inc(pg_idx, 1)
                    dve.wait_ge(pg_idx, 5)
                    nc.vector.tensor_copy(page_idx[:, :], pagef[:, :]).then_inc(pg_idx, 1)
                    dve.wait_ge(dq_ps, 1)
                    bm = dc["bm4"].unsqueeze(1).to_broadcast([P, 2, 4])
                    nc.vector.scalar_tensor_tensor(wsel[:, :, :], PS[3][:, 640:648].rearrange("p (a j) -> p a j", a=2),
                                                   float(H ** -0.5), bm, ALU.mult, ALU.mult).then_inc(dq_got, 1)
                    for it in range(8):
                        dve.wait_ge(kx_sum, it + 1)
                        bg, gp = it // 4, it % 4
                        dst = SC[:, 4 * bg:4 * bg + 4, 8 * gp:8 * gp + 8].rearrange("p j (g q r) -> p j g q r", g=2, q=2)
                        src = PS[3][:, 512:544].rearrange("p (r g q j) -> p j g q r", r=2, g=2, q=2)
                        for g2 in range(2):
                            ins = nc.vector.tensor_copy(dst[:, :, g2], src[:, :, g2])
                        ins.then_inc(kx_got, 1)
                    dve.wait_ge(dx_pe, 2)
                    nc.vector.tensor_copy(SC[0:1, :, 32], PS[3][0:1, 0:8]).then_inc(dx_dve, 1)

                @block.scalar
                def _(act):
                    act.wait_ge(dq_ps, 1)
                    for r in range(2):
                        nc.scalar.activation(qix[:, :, :].rearrange("p b (m r) -> p r m b", r=2)[:, r],
                                             PS[3][:, 32 * r:32 * r + 32].rearrange("p (m b) -> p m b", m=4), ACT.Copy)\
                            .then_inc(dx_act, 1)
                    for it in range(8):
                        for j in range(4):
                            act.wait_ge(kx_ps, 4 * it + j + 1)
                            if it >= 2:
                                act.wait_ge(kx_sc, it - 1)
                            nc.scalar.activation(kxT[:, it % 2, j], PS[j // 2][:, 512 * (j % 2):512 * (j % 2) + 512], ACT.Copy)\
                                .then_inc(kx_T, 1)
                        act.wait_ge(kx_sc, it + 1)
                        if it >= 2:
                            act.wait_ge(kx_sum, it - 1)
                        nc.scalar.activation(rx[:, it % 2], PS[2][:, :], ACT.Relu, scale=0.125).then_inc(kx_relu, 1)
                    act.wait_ge(dx_pe, 1)
                    nc.scalar.activation(rn[:, :], PS[2][:, 0:2], ACT.Relu, scale=0.125).then_inc(dx_act, 1)

                @block.tensor
                def _(pe):
                    pe.wait_ge(dc_in, 16)
                    for r, name in ((0, "even"), (1, "odd")):
                        nc.tensor.matmul(PS[3][:, 32 * r:32 * r + 32], cst[name], qiT[:, :, LP:], start=True, stop=True)
                    nc.tensor.matmul(PS[3][:, 640:648], dc["hsel"][64:72, :], abT[64:72, LP:], start=True, stop=True)\
                        .then_inc(dq_ps, 1)
                    pe.wait_ge(dx_act, 2)
                    pe.wait_ge(dq_got, 1)

                    def transposes(it):
                        for j in range(4):
                            if it:
                                pe.wait_ge(kx_T, 4 * (it - 1) + j + 1)
                            for g2 in range(2):
                                i = 8 * it + 2 * j + g2
                                pe.wait_ge(kx_sem[i % NKX], 16 * (i // NKX + 1))
                                for q in range(2):
                                    mm = nc.tensor.transpose(
                                        PS[j // 2][:, 512 * (j % 2) + 256 * g2 + P * q:512 * (j % 2) + 256 * g2 + P * q + P],
                                        kx[:, i % NKX, P * q:P * q + P], cst["ident"])
                            mm.then_inc(kx_ps, 1)

                    transposes(0)
                    for it in range(8):
                        bg = it // 4
                        if it + 1 < 8:
                            transposes(it + 1)
                        pe.wait_ge(kx_T, 4 * it + 4)
                        if it:
                            pe.wait_ge(kx_relu, it)
                        for r in range(2):
                            for j in range(4):
                                rp = slice(64 * r, 64 * r + 64)
                                mm = nc.tensor.matmul(PS[2][32 * j:32 * j + 8, 512 * r:512 * r + 512], qix[rp, 4 * bg + j, :],
                                                      kxT[rp, it % 2, j], start=True, stop=True,
                                                      tile_position=(64 * r, 32 * j))
                        mm.then_inc(kx_sc, 1)
                        pe.wait_ge(kx_relu, it + 1)
                        if it:
                            pe.wait_ge(kx_got, it)
                        for c in range(8):
                            mm = nc.tensor.matmul(PS[3][:, 512 + 4 * c:516 + 4 * c], rx[:, it % 2, P * c:P * c + P],
                                                  wsel[:, bg, :], start=True, stop=True)
                        mm.then_inc(kx_sum, 1)
                    for b in range(NS):
                        j, bg = b % 4, b // 4
                        mm = nc.tensor.matmul(PS[2][32 * j:32 * j + 8, bg:bg + 1], qix[0:64, b, :], kiT[0:64, LP + b:LP + b + 1],
                                              start=True, stop=True, tile_position=(0, 32 * j))
                    mm.then_inc(dx_pe, 1)
                    pe.wait_ge(dx_act, 3)
                    for bg in range(2):
                        mm = nc.tensor.matmul(PS[3][0:1, 4 * bg:4 * bg + 4], rn[:, bg:bg + 1], wsel[:, bg, :], start=True, stop=True)
                    mm.then_inc(dx_pe, 1)

        names = ("bs_dve", "bs_cnt", "bs_tot", "sr_dve", "sr_pe")
        bs_dve, bs_cnt, bs_tot, sr_dve, sr_pe = (sem(n) for n in names)
        NKEY = PAST + 1
        BITS = 31
        with ExitStack() as scope:
            Z = sb("Z", [P, NS, 33], scope=scope)
            ge = sb("ge", [P, NS, 33], scope=scope)
            cnt = sb("cnt", [P, NS], BF16, scope)
            onesb = sb("onesb", [P, P], BF16, scope)
            cur, cand, bit, keep = (sb(n, [P, NS], I32, scope) for n in ("cur", "cand", "bit", "keep"))
            pos, sign, kth, thr, need = (sb(n, [P, NS], scope=scope) for n in ("pos", "sign", "kth", "thr", "need"))
            EQ, SEL, GT = (sb(n, [P, NS, 33], scope=scope) for n in ("EQ", "SEL", "GT"))
            part = sb("part", [P, 64], scope=scope)
            pre = sb("pre", [P, 64, 4], scope=scope)
            base = sb("base", [P, 64], scope=scope)
            ranki, hii, loi = (sb(n, [P, 256], I32, scope) for n in ("ranki", "hii", "loi"))
            hif, lof = sb("hif", [P, 256], scope=scope), sb("lof", [P, 256], scope=scope)
            hot_hi = sb("hot_hi", [P, 256, 16], scope=scope)
            hot_lo = sb("hot_lo", [P, 256, 2, 16], scope=scope)
            rowid = sb("rowid", [P, 64, 4], scope=scope)
            slots = sb("slots", [P, 2, 2, 16], scope=scope)
            back = sb("back", [32, P], scope=scope)
            with nc.Block() as block:
                @block.vector
                def _(dve):
                    link, V = chain_dve.link, nc.vector

                    def along(ap, n=33):
                        return ap.unsqueeze(2).to_broadcast([P, NS, n])

                    link(dve, V.memset(onesb[:, :], 1.0))
                    link(dve, V.memset(cur[:, :], 0))
                    link(dve, V.memset(bit[:, :], 1 << (BITS - 1)))
                    link(dve, V.tensor_scalar(ge[:, :, :], SC[:, :, :], 0.0, None, ALU.is_ge))
                    with nc.allow_low_precision(reason="counts up to 33 are exact"):
                        V.tensor_reduce(cnt[:, :], ge[:, :, :], AXX, ALU.add).then_inc(bs_cnt, 1)
                    dve.wait_ge(bs_tot, 1)
                    tot = PS[0][:, 0:NS]
                    link(dve, V.tensor_scalar(pos[:, :], tot, float(TOPK_S), None, ALU.is_ge))
                    link(dve, V.tensor_scalar(sign[:, :], pos[:, :], 2.0, -1.0, ALU.mult, ALU.add))
                    link(dve, V.tensor_scalar(kth[:, :], pos[:, :], float(TOPK_S - (NKEY - TOPK_S + 1)),
                                              float(NKEY - TOPK_S + 1), ALU.mult, ALU.add))
                    link(dve, V.tensor_tensor(Z[:, :, 0:32], SC[:, :, 0:32], along(sign[:, :], 32), ALU.mult))
                    link(dve, V.memset(Z[:, :, 32:33], FAR))
                    link(dve, V.tensor_tensor(Z[0:1, :, 32], SC[0:1, :, 32], sign[0:1, :], ALU.mult))
                    with dve.Fori(0, BITS) as i:
                        V.tensor_tensor(cand[:, :], cur[:, :], bit[:, :], ALU.bitwise_or).then_inc(bs_dve, 1)
                        dve.wait_ge(bs_dve, i * 6 + 1)
                        V.tensor_tensor(ge[:, :, :], Z[:, :, :], along(cand[:, :].bitcast(F32)), ALU.is_ge).then_inc(bs_dve, 1)
                        dve.wait_ge(bs_dve, i * 6 + 2)
                        with nc.allow_low_precision(reason="counts up to 33 are exact"):
                            V.tensor_reduce(cnt[:, :], ge[:, :, :], AXX, ALU.add).then_inc(bs_cnt, 1)
                        V.tensor_scalar(bit[:, :], bit[:, :], 1, None, ALU.logical_shift_right).then_inc(bs_dve, 1)
                        dve.wait_ge(bs_tot, i + 2)
                        V.tensor_tensor(keep[:, :], tot, kth[:, :], ALU.is_ge).then_inc(bs_dve, 1)
                        dve.wait_ge(bs_dve, i * 6 + 4)
                        V.copy_predicated(cur[:, :], keep[:, :], cand[:, :]).then_inc(bs_dve, 2)
                        dve.wait_ge(bs_dve, i * 6 + 6)
                    link(dve, V.tensor_tensor(thr[:, :], cur[:, :].bitcast(F32), sign[:, :], ALU.mult))
                    link(dve, V.tensor_tensor(GT[:, :, :], SC[:, :, :], along(thr[:, :]), ALU.is_gt))
                    link(dve, V.tensor_tensor(EQ[:, :, :], SC[:, :, :], along(thr[:, :]), ALU.is_equal))

                    def ranks(marks, n_pe):
                        m4 = marks[:, :, 0:32].rearrange("p b (g s) -> p b g s", s=4)
                        V.tensor_reduce(part[:, :].rearrange("p (b g) -> p b g", b=NS), m4, AXX, ALU.add).then_inc(sr_dve, 1)
                        p4 = pre[:, :, :].rearrange("p (b g) s -> p b g s", b=NS)
                        link(dve, V.memset(pre[:, :, 0:1], 0.0))
                        for s in range(3):
                            link(dve, V.tensor_tensor(p4[:, :, :, s + 1], p4[:, :, :, s], m4[:, :, :, s], ALU.add))
                        dve.wait_ge(sr_pe, n_pe)
                        totals = PS[1][:, 0:64]
                        link(dve, V.tensor_copy(part[:, :], totals))
                        link(dve, V.tensor_tensor_scan(base[:, :], dc["gres"], part[:, :], 0.0, ALU.mult, ALU.add))
                        link(dve, V.tensor_tensor(base[:, :], base[:, :], part[:, :], ALU.subtract))
                        link(dve, V.tensor_tensor(base[:, :], base[:, :], PS[1][:, 512:576], ALU.add))
                        link(dve, V.tensor_tensor(pre[:, :, :], pre[:, :, :],
                                                  base[:, :].unsqueeze(2).to_broadcast([P, 64, 4]), ALU.add))

                    V.tensor_reduce(need[:, :], GT[:, :, :], AXX, ALU.add).then_inc(sr_dve, 1)
                    ranks(EQ, 2)
                    link(dve, V.tensor_scalar(need[:, :], PS[0][:, 0:NS], -1.0, float(TOPK_S), ALU.mult, ALU.add))
                    past = pre[:, :, :].rearrange("p (b g) s -> p b (g s)", b=NS)
                    link(dve, V.tensor_tensor(SEL[:, :, 0:32], past, along(need[:, :], 32), ALU.is_lt))
                    link(dve, V.tensor_reduce(kth[:, :], part[:, :].rearrange("p (b g) -> p b g", b=NS), AXX, ALU.add))
                    link(dve, V.tensor_tensor(SEL[:, :, 32], kth[:, :], need[:, :], ALU.is_lt))
                    link(dve, V.tensor_tensor(SEL[:, :, :], SEL[:, :, :], EQ[:, :, :], ALU.mult))
                    link(dve, V.tensor_tensor(SEL[:, :, :], SEL[:, :, :], GT[:, :, :], ALU.add))
                    link(dve, V.tensor_copy(selnew[:, :], SEL[:, :, 32]))
                    ranks(SEL, 3)
                    link(dve, V.tensor_scalar(hif[:, :].rearrange("p (b c) -> p b c", b=NS), SEL[:, :, 0:32], -1024.0, 1024.0,
                                              ALU.mult, ALU.add))
                    link(dve, V.tensor_tensor(ranki[:, :], pre[:, :, :].rearrange("p c s -> p (c s)"), hif[:, :], ALU.add))
                    link(dve, V.tensor_scalar(hii[:, :], ranki[:, :], 4, None, ALU.logical_shift_right))
                    link(dve, V.tensor_scalar(loi[:, :], ranki[:, :], 15, None, ALU.bitwise_and))
                    link(dve, V.tensor_copy(hif[:, :], hii[:, :]))
                    link(dve, V.tensor_copy(lof[:, :], loi[:, :]))
                    io = dc["iota16"].unsqueeze(1).to_broadcast([P, 256, 16])
                    V.tensor_tensor(hot_hi[:, :, :], io, hif[:, :].unsqueeze(2).to_broadcast([P, 256, 16]), ALU.is_equal)\
                        .then_inc(sr_dve, 1)
                    link(dve, V.tensor_tensor(hot_lo[:, :, 0], io, lof[:, :].unsqueeze(2).to_broadcast([P, 256, 16]), ALU.is_equal))
                    link(dve, V.tensor_scalar(base[:, :], pagef[:, :], 4.0, None, ALU.mult))
                    for s in range(4):
                        link(dve, V.tensor_scalar(rowid[:, :, s], base[:, :], float(s), None, ALU.add))
                    rid = rowid[:, :, :].rearrange("p c s -> p (c s)")
                    for v, val in ((1, dc["kpos"]), (0, rid)):
                        V.tensor_tensor(hot_lo[:, :, v], hot_lo[:, :, 0], val.unsqueeze(2).to_broadcast([P, 256, 16]), ALU.mult)\
                            .then_inc(sr_dve, 1)
                    dve.wait_ge(sr_pe, 4)
                    V.tensor_copy(slots[:, :, :, :].rearrange("p a v l -> p (a v l)"), PS[2][:, 0:64]).then_inc(sr_dve, 1)
                    dve.wait_ge(sr_pe, 5)
                    V.tensor_copy(ridx[:, :, :].rearrange("p f b -> p (f b)"), PS[3][:, 0:16]).then_inc(sr_dve, 1)
                    V.tensor_copy(posf[:, :, :].rearrange("p f b -> p (f b)"), PS[3][:, 16:32]).then_inc(sr_dve, 1)
                    dve.wait_ge(sr_dve, 9)

                @block.tensor
                def _(pe):
                    pe.wait_ge(bs_cnt, 1)
                    nc.tensor.matmul(PS[0][:, 0:NS], onesb[:, :], cnt[:, :], start=True, stop=True).then_inc(bs_tot, 1)
                    with pe.Fori(0, BITS) as i:
                        pe.wait_ge(bs_cnt, i + 2)
                        nc.tensor.matmul(PS[0][:, 0:NS], onesb[:, :], cnt[:, :], start=True, stop=True).then_inc(bs_tot, 1)
                    pe.wait_ge(sr_dve, 1)
                    nc.tensor.matmul(PS[0][:, 0:NS], cst["ones"], need[:, :], start=True, stop=True).then_inc(sr_pe, 1)
                    for w in (2, 3):
                        pe.wait_ge(sr_dve, w)
                        nc.tensor.matmul(PS[1][:, 0:64], cst["ones"], part[:, :], start=True, stop=True)
                        nc.tensor.matmul(PS[1][:, 512:576], cst["strict"], part[:, :], start=True, stop=True).then_inc(sr_pe, 1)
                    pe.wait_ge(sr_dve, 6)
                    for c in range(32):
                        for b in range(NS):
                            j, bg = b % 4, b // 4
                            mm = nc.tensor.matmul(PS[2][32 * j:32 * j + 16, 32 * bg:32 * bg + 32], hot_hi[:, 32 * b + c],
                                                  hot_lo[:, 32 * b + c].rearrange("p v l -> p (v l)"),
                                                  start=c == 0 and bg == 0, stop=c == 31, tile_position=(0, 32 * j),
                                                  skip_group_check=True)
                    mm.then_inc(sr_pe, 1)
                    pe.wait_ge(sl_back, 64)
                    nc.tensor.transpose(PS[3][:, 0:32], back[:, :], cst["ident"][:32, :32]).then_inc(sr_pe, 1)

                @block.sync
                def _(sp):
                    sp.wait_ge(sr_dve, 7)
                    for j in range(4):
                        for bg in range(2):
                            dst = slots_dram.ap()[:, 4 * bg + j].rearrange("v (h l) -> h v l", l=16)
                            sp.dma_start(dst, slots[32 * j:32 * j + 16, bg]).then_inc(sl_out, 16)
                    sp.wait_ge(sl_out, 16 * 8)
                    for v in range(2):
                        for f in range(2):
                            sp.dma_start(back[16 * v + 8 * f:16 * v + 8 * f + 8, :],
                                         slots_dram.ap()[v, :, P * f:P * f + P]).then_inc(sl_back, 16)


        names = ("at_pe", "at_act", "at_dve", "q_bc", "rb_zero", "rb_in", "exp_done")
        at_pe, at_act, at_dve, q_bc, rb_zero, rb_in, exp_done = (sem(n) for n in names)
        NKS = 4
        k_in = [sem(f"k_in{i}") for i in range(NKS)]
        v_in = sem("v_in")
        with ExitStack() as scope:
            kg = sb("kg", [P, NKS, 512], scope=scope)
            vg = sb("vg", [P, 2 * NS, 512], scope=scope)
            qtok = sb("qtok", [NS, 512], scope=scope)
            prod = sb("prod", [P, 512], scope=scope)
            lg = sb("lg", [P, 2, NS, H], scope=scope)
            lgnew = sb("lgnew", [NS, H], scope=scope)
            hot = sb("hot", [P, 2, NS, 32], scope=scope)
            hotT = sb("hotT", [P, 512], scope=scope)
            rbblk = sb("rbblk", [P, 2, 64], scope=scope)
            rb0 = sb("rb0", [64, 1], scope=scope)
            biasS = sb("biasS", [64, 256], scope=scope)
            Lg, Pd = sb("Lg", [64, 257], scope=scope), sb("Pd", [64, 257], scope=scope)
            st = sb("st", [64, 8], scope=scope)
            n8 = sb("n8", [64, 8], scope=scope)
            selx = sb("selx", [P, NS, H], scope=scope)
            PTd = sb("PTd", [P, 2, 64], scope=scope)
            t32, v32 = sb("t32", [64, 32], scope=scope), sb("v32", [P, 32], scope=scope)
            mv = sb("mv", [P, 2, 512], scope=scope)
            with nc.Block() as block:
                @block.gpsimd
                def _(pool):
                    for name, i0 in (("cache_b_k", 0), ("cache_b_v", 1)):
                        src = d[name][0].rearrange("n r h e -> (n r) (h e)")
                        for i in range(2 * NS):
                            b, f = i // 2, i % 2
                            off = bass.IndirectOffsetOnAxis(ap=ridx[:, f, b:b + 1], axis=0)
                            if i0 == 0:
                                if i >= NKS:
                                    pool.wait_ge(k_used, i - NKS + 1)
                                pool.indirect_dma_start(kg[:, i % NKS], None, src, off).then_inc(k_in[i % NKS], 16)
                            else:
                                pool.indirect_dma_start(vg[:, i], None, src, off).then_inc(v_in, 16)

                @block.sync
                def _(sp):
                    sp.wait_ge(rb_zero, 1)
                    for b in range(NS):
                        sp.dma_start(rbblk[32 * (b % 4):32 * (b % 4) + 32, b // 4, 8 * b:8 * b + 8], d["rel_bias"]).then_inc(rb_in, 16)
                    with nc.allow_non_contiguous_dma(reason="64 single values"):
                        sp.dma_start(rb0[:, :], bass.AP(tensor=d["rel_bias"].tensor, offset=0, ap=[[0, NS], [1, H]])
                                     .unsqueeze(2)).then_inc(rb_in, 16)

                @block.tensor
                def _(pe):
                    ident = cst["ident"]
                    for a in range(4):
                        nc.tensor.transpose(PS[0][0:NS, P * a:P * a + P], qbT[:, a, LP:], ident)
                        mm = nc.tensor.transpose(PS[1][0:NS, P * a:P * a + P], kbT[:, a, LP:], ident)
                    mm.then_inc(at_pe, 1)
                    pe.wait_ge(at_act, 1)
                    for b in range(NS):
                        if b >= 2:
                            pe.wait_ge(k_used, 2 * (b - 1))
                        nc.tensor.matmul(PS[2 + b % 2][:, 0:512], sel_h[0:8, b, :], qtok[:, :], start=True, stop=True)\
                            .then_inc(q_bc, 1)
                    pe.wait_ge(at_dve, 3)
                    for f in range(2):
                        for bg in range(2):
                            mm = nc.tensor.transpose(PS[1][:, 512 + 256 * f + P * bg:512 + 256 * f + P * bg + P],
                                                     hot[:, f, 4 * bg:4 * bg + 4].rearrange("p b j -> p (b j)"), ident)
                    mm.then_inc(at_pe, 1)
                    pe.wait_ge(at_act, 2)
                    pe.wait_ge(rb_in, 16 * 9)
                    for f in range(2):
                        for bg in range(2):
                            mm = nc.tensor.matmul(PS[0][0:64, 512 + P * f:512 + P * f + P], rbblk[:, bg],
                                                  hotT[:, 256 * f + P * bg:256 * f + P * bg + P], start=bg == 0, stop=bg == 1)
                    mm.then_inc(at_pe, 1)
                    pe.wait_ge(k_used, 2 * NS)
                    nc.tensor.matmul(PS[3][0:64, 0:8], dc["e64"][0:8, :], lgnew[:, :], start=True, stop=True)
                    nc.tensor.matmul(PS[3][0:64, 8:9], selx[:, :, :].rearrange("p b h -> p (b h)"), cst["ones"][:, 0:1],
                                     start=True, stop=True)
                    for f in range(2):
                        mm = nc.tensor.transpose(PS[0][0:64, P * f:P * f + P], lg[:, f].rearrange("p b h -> p (b h)"), ident)
                    mm.then_inc(at_pe, 1)
                    pe.wait_ge(at_dve, 5)
                    for f in range(2):
                        nc.tensor.transpose(PS[1][:, 64 * f:64 * f + 64], Pd[:, P * f:P * f + P], ident[:64, :64])
                    nc.tensor.matmul(PS[3][:, 64:96], dc["parsel"][0:64, :], t32[:, :], start=True, stop=True)\
                        .then_inc(at_pe, 1)
                    pe.wait_ge(at_act, 4)
                    pe.wait_ge(v_in, 16 * 2 * NS)
                    for i in range(2 * NS):
                        b, f = i // 2, i % 2
                        mm = nc.tensor.matmul(PS[2][32 * (b % 4):32 * (b % 4) + 8, 512 * (b // 4):512 * (b // 4) + 512],
                                              PTd[:, f, 8 * b:8 * b + 8], vg[:, i], start=f == 0, stop=f == 1,
                                              tile_position=(0, 32 * (b % 4)), skip_group_check=True)
                    mm.then_inc(at_pe, 1)
                    pe.wait_ge(at_dve, 6)
                    for bg in range(2):
                        for a in range(4):
                            mm = nc.tensor.matmul(PS[0][:, 8 * a + 4 * bg:8 * a + 4 * bg + 4], mv[:, bg, P * a:P * a + P],
                                                  dc["bm4"], start=True, stop=True)
                    mm.then_inc(at_pe, 1)

                @block.scalar
                def _(act):
                    act.wait_ge(at_pe, 1)
                    nc.scalar.activation(qtok[:, :], PS[0][0:NS, 0:512], ACT.Copy).then_inc(at_act, 1)
                    act.wait_ge(at_pe, 2)
                    nc.scalar.activation(hotT[:, :], PS[1][:, 512:1024], ACT.Copy).then_inc(at_act, 1)
                    act.wait_ge(at_pe, 3)
                    nc.scalar.activation(biasS[:, :], PS[0][0:64, 512:768], ACT.Copy).then_inc(at_act, 1)
                    act.wait_ge(at_dve, 4)
                    nc.scalar.activation(Pd[:, :], Lg[:, :], ACT.Exp, bias=st[:, 0:1], accum_out=st[:, 1:2])\
                        .then_inc(exp_done, 1)
                    act.wait_ge(at_pe, 5)
                    nc.scalar.activation(PTd[:, :, :].rearrange("p f c -> p (f c)"), PS[1][:, 0:128], ACT.Copy)\
                        .then_inc(at_act, 1)

                @block.vector
                def _(dve):
                    link, V = chain_dve.link, nc.vector
                    V.memset(rbblk[:, :, :], 0.0).then_inc(rb_zero, 1)
                    link(dve, V.tensor_scalar(posf[:, :, :], posf[:, :, :], -1.0, float(PAST), ALU.mult, ALU.add))
                    dist = posf[:, :, :].unsqueeze(3).to_broadcast([P, 2, NS, 32])
                    thr = dc["thr"].unsqueeze(1).unsqueeze(1).to_broadcast([P, 2, NS, 32])
                    link(dve, V.tensor_tensor(hot[:, :, :, :], dist, thr, ALU.is_ge))
                    V.tensor_tensor(hot[:, :, :, 0:31], hot[:, :, :, 0:31], hot[:, :, :, 1:32], ALU.subtract).then_inc(at_dve, 1)
                    dve.wait_ge(at_act, 1)
                    link(dve, V.tensor_tensor(prod[0:NS, :], qtok[:, :], PS[1][0:NS, 0:512], ALU.mult))
                    V.tensor_reduce(lgnew[:, :], prod[0:NS, :].rearrange("p (h e) -> p h e", h=H), AXX, ALU.add).then_inc(at_dve, 1)
                    V.tensor_copy(selx[:, :, :], selnew[:, :].unsqueeze(2).to_broadcast([P, NS, H])).then_inc(at_dve, 1)
                    dve.wait_ge(at_dve, 3)
                    for i in range(2 * NS):
                        b, f = i // 2, i % 2
                        dve.wait_ge(q_bc, b + 1)
                        dve.wait_ge(k_in[i % NKS], 16 * (i // NKS + 1))
                        link(dve, V.tensor_tensor(prod[:, :], kg[:, i % NKS], PS[2 + b % 2][:, 0:512], ALU.mult))
                        V.tensor_reduce(lg[:, f, b], prod[:, :].rearrange("p (h e) -> p h e", h=H), AXX, ALU.add)\
                            .then_inc(k_used, 1)
                        dve.wait_ge(k_used, i + 1)
                    dve.wait_ge(at_pe, 4)
                    dve.wait_ge(at_act, 3)
                    V.scalar_tensor_tensor(Lg[:, 0:256], PS[0][0:64, 0:256], 0.125, biasS[:, :], ALU.mult, ALU.add)\
                        .then_inc(chain_dve.sem, 1)
                    chain_dve.n += 1
                    link(dve, V.tensor_tensor(n8[:, :], PS[3][0:64, 0:8], dc["hm8"][0:64, :], ALU.mult))
                    link(dve, V.tensor_reduce(st[:, 2:3], n8[:, :], AXX, ALU.add))
                    link(dve, V.tensor_scalar(Lg[:, 256:257], st[:, 2:3], 0.125, rb0[:, 0:1], ALU.mult, ALU.add))
                    link(dve, V.tensor_scalar(st[:, 3:4], PS[3][0:64, 8:9], NEG, None, ALU.mult))
                    link(dve, V.tensor_scalar(st[:, 4:5], PS[3][0:64, 8:9], -NEG, NEG, ALU.mult, ALU.add))
                    link(dve, V.tensor_tensor(Lg[:, 255:257], Lg[:, 255:257], st[:, 3:5], ALU.add))
                    V.tensor_reduce(st[:, 0:1], Lg[:, :], AXX, ALU.max, negate=True).then_inc(at_dve, 1)
                    dve.wait_ge(exp_done, 1)
                    link(dve, V.reciprocal(st[:, 5:6], st[:, 1:2]))
                    link(dve, V.tensor_scalar(Pd[:, :], Pd[:, :], st[:, 5:6], None, ALU.mult))
                    V.tensor_scalar(t32[:, :], dc["maskA"][0:64, :], Pd[:, 256:257], None, ALU.mult).then_inc(at_dve, 1)
                    dve.wait_ge(at_pe, 6)
                    hm = dc["hmask"].unsqueeze(2).to_broadcast([P, H, DH])
                    for bg in range(2):
                        ins = V.tensor_tensor(mv[:, bg].rearrange("p (h e) -> p h e", h=H),
                                              PS[2][:, 512 * bg:512 * bg + 512].rearrange("p (h e) -> p h e", h=H), hm, ALU.mult)
                        if bg == 0:
                            link(dve, ins)
                    ins.then_inc(at_dve, 1)
                    vnew_ = vbT[:, :, LP:]
                    link(dve, V.tensor_tensor(v32[:, :].rearrange("p (m b) -> p m b", m=4), vnew_,
                                              PS[3][:, 64:96].rearrange("p (m b) -> p m b", m=4), ALU.mult))
                    dve.wait_ge(at_pe, 7)
                    link(dve, V.tensor_tensor(oT[:, 4:8, LP:], v32[:, :].rearrange("p (m b) -> p m b", m=4),
                                              PS[0][:, 0:32].rearrange("p (m b) -> p m b", m=4), ALU.add))
        L0.close()

        GROUPS = DFF // D
        relu_done, sqr_done, hid_hi_done, hid_done = (sem(n) for n in ("relu_done", "sqr_done", "hid_hi_done", "hid_done"))

        def mlp_jobs(layer):
            up = d["w_up"][layer].rearrange("(k p) c -> p k c", p=P)
            down = d["w_down"][layer].rearrange("(k p) c -> p k c", p=P)
            n0 = len(jobs)
            for g in range(GROUPS):
                for m in range(KT):
                    add_job([(0, up[:, :, (KT * g + m) * P:(KT * g + m + 1) * P])])
                for m in range(KT):
                    add_job([(0, down[:, KT * g:KT * g + KT, m * P:(m + 1) * P])])
            return n0

        def mlp(layer, n0, x_hi, x_lo, hid_hi, hid_lo, next_jobs, tail_of=None):
            up = d["w_up"][layer].rearrange("(k p) c -> p k c", p=P)
            down = d["w_down"][layer].rearrange("(k p) c -> p k c", p=P)
            per = 2 * KT
            base = 2 + GROUPS * KT * layer
            tmp, sqr = oT[:, 0:2], oT[:, 2:4]
            LAST = GROUPS - 1
            assert per % NRAW == 0

            def groups(eng, body):
                with eng.Fori(0, LAST) as i:
                    body(i, True)
                body(LAST, False)

            with nc.Block() as block:
                @block.sync
                def _(sp):
                    def body(i, more):
                        for m in range(KT):
                            load_job(sp, n0 + m, up[:, :, bass.ds(i * D + m * P, P)], i, per)
                        for m in range(KT):
                            load_job(sp, n0 + KT + m, down[:, bass.ds(i * KT, KT), m * P:(m + 1) * P], i, per)
                    groups(sp, body)
                    loaded[0] = n0 + GROUPS * per
                    load_weights(sp, loaded[0] + next_jobs)

                @block.scalar
                def _(act):
                    split_high(act, n0)

                    def body(i, more):
                        for j in range(per):
                            n = n0 + j
                            if more or j + 1 < per:
                                split_high(act, n + 1, i, per)
                            if j < KT:
                                u = i * KT + (base + j)
                                act.wait_ge(gemm_done, i * per + (n + 1))
                                act.wait_ge(hid_done, u - 1)
                                nc.scalar.activation(halves(tmp[:, j % 2]), job_psum(n), ACT.Relu).then_inc(psum_free[n % 2], 1)
                                act.wait_ge(psum_free[n % 2], i * (per // 2) + (n // 2 + 1))
                                nc.scalar.activation(hid_hi[:, j], tmp[:, j % 2], ACT.Square).then_inc(hid_hi_done, 1)
                    groups(act, body)

                @block.gpsimd
                def _(pool):
                    if layer == 0:
                        pool.memset(vec[:, SPARE:SPARE + 1], 0.0).then_inc(sqr_done, 1)
                        pool.memset(vec[:, SPARE + 1:SPARE + 2], 0.0).then_inc(sqr_done, 1)

                    def body(i, more):
                        for j in range(KT):
                            n = n0 + j
                            u = i * KT + (base + j)
                            pool.wait_ge(psum_free[n % 2], i * (per // 2) + (n // 2 + 1))
                            pool.wait_ge(hid_done, u - 1)
                            nc.gpsimd.tensor_tensor(sqr[:, j % 2], tmp[:, j % 2], tmp[:, j % 2], ALU.mult).then_inc(sqr_done, 1)
                    groups(pool, body)

                @block.vector
                def _(dve):
                    if layer == 0:
                        nc.vector.memset(vec[:, SPARE + 2:SPARE + 3], 0.0).then_inc(hid_done, 1)
                        nc.vector.memset(vec[:, SPARE + 3:SPARE + 4], 0.0).then_inc(hid_done, 1)
                    split_low(dve, n0)

                    def body(i, more):
                        for j in range(per):
                            n = n0 + j
                            if more or j + 1 < per:
                                split_low(dve, n + 1, i, per)
                            if j < KT:
                                u = i * KT + (base + j)
                                dve.wait_ge(hid_hi_done, u - 1)
                                dve.wait_ge(sqr_done, u + 1)
                                nc.vector.tensor_tensor(hid_lo[:, j], sqr[:, j % 2], hid_hi[:, j].bitcast(F32), ALU.subtract)\
                                    .then_inc(hid_done, 1)
                            else:
                                add_to_residual(dve, n, j - KT, i, per)
                    groups(dve, body)

                @block.tensor
                def _(pe):
                    def body(i, more):
                        for j in range(KT):
                            multiply(pe, n0 + j, x_hi, x_lo, None, i, per)
                        for j in range(KT):
                            ready = (lambda k: pe.wait_ge(hid_done, i * KT + (base + k + 1))) if j == 0 else None
                            multiply(pe, n0 + KT + j, hid_hi, hid_lo, ready, i, per)
                    groups(pe, body)

        JM0 = mlp_jobs(0)
        w_in_c = d["w_in_c"][0].rearrange("(k p) c -> p k c", p=P)
        JC = blocks(d["w_in_c"][0], 0, QL + KV)
        JKPE = add_job([(ROPE * r, w_in_c[:, :, QL + KV:QL + KV + ROPE]) for r in range(4)])

        def out_projection(js, x_hi, x_lo, sp_act, sp_dve, wcol, next_jobs):
            last = js[0]
            n_act, n_pe, n_dve = norm(hT, KT, D, wcol, x_hi, x_lo,
                                      before=lambda act, k: act.wait_ge(psum_free[js[k] % 2], js[k] // 2 + 1))
            with nc.Block() as block:
                @block.sync
                def _(sp):
                    load_weights(sp, js[-1] + 1)

                @block.scalar
                def _(act):
                    sp_act(act)
                    for n in js:
                        split_high(act, n)
                    n_act(act)

                @block.vector
                def _(dve):
                    sp_dve(dve)
                    for n in js:
                        split_low(dve, n)
                        if n > js[0]:
                            add_to_residual(dve, n - 1, n - 1 - js[0])
                    add_to_residual(dve, js[-1], KT - 1)
                    n_dve(dve)

                @block.tensor
                def _(pe):
                    pe.wait_ge(lo_ready, lo_before + KT)
                    for n in js:
                        multiply(pe, n, x_hi, x_lo)
                    n_pe(pe)

        with ExitStack() as scope:
            x_hi, x_lo = sb("x_hi", [P, KT, TOK], F32R, scope), sb("x_lo", [P, KT, TOK], F32R, scope)
            lo_before = count["tile"]
            sp_act, sp_dve = split(oT, KT, x_hi, x_lo)
            out_projection(JO, x_hi, x_lo, sp_act, sp_dve, FFN1, 0)
            hid_hi, hid_lo = sb("hid_hi", [P, KT, TOK], F32R, scope), sb("hid_lo", [P, KT, TOK], F32R, scope)
            mlp(0, JM0, x_hi, x_lo, hid_hi, hid_lo, 6)

        w_uq = d["w_uq_c"][0].rearrange("(k p) c -> p k c", p=P)
        QH = DH + ROPE
        JNOPE = [add_job([(DH * e, w_uq[:, :, (2 * a + e) * QH:(2 * a + e) * QH + DH]) for e in range(2)], QL // P)
                 for a in range(4)]
        JPE = [add_job([(ROPE * e, w_uq[:, :, (4 * a + e) * QH + DH:(4 * a + e + 1) * QH]) for e in range(4)], QL // P)
               for a in range(2)]
        JO1 = blocks(d["w_out_c"][0], 0, D)
        JM1 = mlp_jobs(1)
        L1 = ctx.enter_context(ExitStack())
        cconst = sb("cconst", [P, sum(n for _, n in ROPE_COLS)], scope=L1)
        cc, at = {}, 0
        for name, n in ROPE_COLS:
            cc[name] = cconst[:, at:at + n]
            at += n
        cT, kpeT = sb("cT", [P, 2, TOK], scope=L1), sb("kpeT", [P, TOK], scope=L1)
        ctok, kpetok = sb("ctok", [P, NT, KV], scope=L1), sb("kpetok", [P, NT, ROPE], scope=L1)
        uv = sb("uv", [P, 2, H, VC], scope=L1)
        qlS = sb("qlS", [P, 2, NS, 32], scope=L1)
        qpS = sb("qpS", [P, NS, 32], scope=L1)
        LQ = L1.enter_context(ExitStack())
        qnT, qpT = sb("qnT", [P, 4, TOK], scope=LQ), sb("qpT", [P, 2, TOK], scope=LQ)
        ukT = sb("ukT", [P, 4, 2, P], scope=LQ)
        c_in, lat_pe, lat_act, lat_dve, rot_ps, rot_done = (
            sem(n) for n in ("c_in", "lat_pe", "lat_act", "lat_dve", "rot_ps", "rot_done"))
        with ExitStack() as scope:
            cqT, ckvT = sb("cqT", [P, 3, TOK], scope=scope), sb("ckvT", [P, 2, TOK], scope=scope)
            uk = sb("uk", [P, 2, H * DH], scope=scope)
            x_hi, x_lo = sb("x_hi", [P, KT, TOK], F32R, scope), sb("x_lo", [P, KT, TOK], F32R, scope)
            n_act, n_pe, n_dve = norm(hT, KT, D, NORM2, x_hi, x_lo)
            lo_before = count["tile"]
            q_act, q_pe, q_dve = norm(cqT, 3, QL, QN, x_hi, x_lo)
            k_act, k_pe, k_dve = norm(ckvT, 2, KV, KN, None, None, keep=cT)
            lo_after = count["tile"]
            JIN = JC + [JKPE]
            turned = [(qpT[:, 0], 0), (qpT[:, 1], 1), (kpeT[:, :], 2)]
            rtmp = oT[:, 5:8]

            with nc.Block() as block:
                @block.sync
                def _(sp):
                    sp.dma_start(cconst[:, :], d["rope"]).then_inc(c_in, 16)
                    sp.dma_start(uk[:, :, :], d["w_uk_c"][0].rearrange("(k p) h n -> p k (h n)", p=P)).then_inc(c_in, 16)
                    sp.dma_start(uv[:, :, :, :], d["w_uv_c"][0].rearrange("(k p) h v -> p k h v", p=P)).then_inc(c_in, 16)
                    load_weights(sp, JPE[-1] + 1 + NRAW)

                @block.scalar
                def _(act):
                    n_act(act)
                    split_high(act, JIN[0])
                    for n in JIN:
                        split_high(act, n + 1)
                        act.wait_ge(gemm_done, n + 1)
                        j = n - JIN[0]
                        dst = cqT[:, j] if j < 3 else ckvT[:, j - 3] if j < 5 else kpeT[:, :]
                        nc.scalar.activation(halves(dst), job_psum(n), ACT.Copy).then_inc(psum_free[n % 2], 1)
                    act.wait_ge(psum_free[0], (JKPE + 2) // 2)
                    act.wait_ge(psum_free[1], (JKPE + 1) // 2)
                    act.wait_ge(gemm_done, JKPE + 1)
                    q_act(act)
                    k_act(act)
                    for n in JNOPE + JPE:
                        if n < JPE[-1]:
                            split_high(act, n + 1)
                        act.wait_ge(gemm_done, n + 1)
                        dst = qnT[:, n - JNOPE[0]] if n < JPE[0] else qpT[:, n - JPE[0]]
                        nc.scalar.activation(halves(dst), job_psum(n), ACT.Copy, scale=MLA_SCALE).then_inc(psum_free[n % 2], 1)
                    act.wait_ge(lat_pe, 1)
                    nc.scalar.activation(ukT[:, :, :, :].rearrange("p a k c -> p (a k c)"), PS[3][:, :], ACT.Copy).then_inc(lat_act, 1)
                    act.wait_ge(lat_pe, 2)
                    nc.scalar.activation(ctok[:, 0:4].rearrange("p t c -> p (t c)"), PS[3][:, :], ACT.Copy).then_inc(lat_act, 1)
                    act.wait_ge(lat_pe, 3)
                    nc.scalar.activation(ctok[:META + NS, 4], PS[3][:META + NS, 0:KV], ACT.Copy)
                    nc.scalar.activation(kpetok[:, 0:4].rearrange("p t c -> p (t c)"), PS[3][:, 512:640], ACT.Copy)
                    nc.scalar.activation(kpetok[:META + NS, 4], PS[3][:META + NS, 640:672], ACT.Copy).then_inc(lat_act, 1)
                    act.wait_ge(lat_pe, 4)
                    act.wait_ge(lat_dve, 1)
                    for r in range(4):
                        ins = nc.scalar.activation(
                            qpS[:, :, 0:H].rearrange("p b (a r) -> p r a b", r=4)[:, r],
                            PS[3][:, 16 * r:16 * r + 16].rearrange("p (a b) -> p a b", a=2), ACT.Copy)
                    ins.then_inc(lat_act, 1)

                @block.vector
                def _(dve):
                    link = chain_dve.link
                    n_dve(dve)
                    split_low(dve, JIN[0])
                    for n in JIN:
                        split_low(dve, n + 1)
                    dve.wait_ge(psum_free[0], (JKPE + 2) // 2)
                    dve.wait_ge(psum_free[1], (JKPE + 1) // 2)
                    q_dve(dve)
                    k_dve(dve)
                    for n in JNOPE + JPE:
                        if n < JPE[-1]:
                            split_low(dve, n + 1)
                    nc.vector.memset(qpS[:, :, :], 0.0)
                    nc.vector.memset(qlS[:, :, :, :], 0.0).then_inc(lat_dve, 1)
                    dve.wait_ge(c_in, 48)
                    for i, (x, j) in enumerate(turned):
                        dve.wait_ge(rot_ps, i + 1)
                        link(dve, nc.vector.tensor_tensor(halves(rtmp[:, i]), halves(PS[2][:, :])[:, :, :HALF],
                                                          halves(cc["sin"]), ALU.mult))
                        link(dve, nc.vector.tensor_tensor(x, x, cc["cos"], ALU.mult))
                        nc.vector.tensor_tensor(x, x, rtmp[:, i], ALU.add).then_inc(rot_done, 1)

                @block.tensor
                def _(pe):
                    n_pe(pe)
                    pe.wait_ge(lo_ready, lo_before)
                    for n in JIN:
                        multiply(pe, n, x_hi, x_lo)
                    pe.wait_ge(c_in, 48)
                    for a in range(4):
                        for k in range(2):
                            mm = nc.tensor.transpose(PS[3][:, (2 * a + k) * P:(2 * a + k + 1) * P], uk[:, k, a * P:(a + 1) * P],
                                                     cst["ident"])
                    mm.then_inc(lat_pe, 1)
                    q_pe(pe)
                    k_pe(pe)
                    pe.wait_ge(lo_ready, lo_after)
                    for n in JNOPE + JPE:
                        multiply(pe, n, x_hi, x_lo)
                    pe.wait_ge(lat_act, 1)
                    for t in range(4):
                        for k in range(2):
                            mm = nc.tensor.transpose(PS[3][:, t * KV + k * P:t * KV + k * P + P], cT[:, k, t * P:t * P + P],
                                                     cst["ident"])
                    mm.then_inc(lat_pe, 1)
                    pe.wait_ge(psum_free[0], (JPE[-1] + 2) // 2)
                    pe.wait_ge(psum_free[1], (JPE[-1] + 1) // 2)
                    for i, (x, j) in enumerate(turned):
                        if i:
                            pe.wait_ge(rot_done, i)
                        for s in range(2):
                            mm = nc.tensor.matmul(PS[2][:, 512 * s:512 * s + HALF], cst["swap"], x[:, s * HALF:(s + 1) * HALF],
                                                  start=True, stop=True)
                        mm.then_inc(rot_ps, 1)
                    pe.wait_ge(rot_done, 3)
                    pe.wait_ge(lat_act, 2)
                    for k in range(2):
                        nc.tensor.transpose(PS[3][:META + NS, k * P:k * P + P], cT[:, k, 4 * P:], cst["ident"])
                    for t in range(NT):
                        n = P if t < 4 else META + NS
                        mm = nc.tensor.transpose(PS[3][:n, 512 + ROPE * t:512 + ROPE * t + ROPE], kpeT[0:ROPE, t * P:t * P + n],
                                                 cst["ident"][:ROPE, :ROPE])
                    mm.then_inc(lat_pe, 1)
                    pe.wait_ge(lat_act, 3)
                    for r in range(4):
                        mm = nc.tensor.matmul(PS[3][:, 16 * r:16 * r + 16], cc["rep"][:, P * r:P * r + P], qpT[:, :, LP:],
                                              start=True, stop=True)
                    mm.then_inc(lat_pe, 1)


        tasks, due = [], {}

        def task(kind, h, k, i):
            due.setdefault(i, []).append(len(tasks))
            tasks.append((kind, h, k))

        NP = len(pairs)
        task("query", 0, 0, -1)
        task("query", 0, 1, -1)
        for h in range(H + 1):
            for t in range(NT):
                i = min(NT * h + t, NP)
                if h and t < 2:
                    task("latent", h - 1, t, i)
                if h + 1 < H and t in (2, 3):
                    task("query", h + 1, t - 2, i)
                if h and t == 4:
                    task("value", h - 1, 0, i)
        mla_task, mla_evac = sem("mla_task"), sem("mla_evac")
        A0 = NP
        with ExitStack() as scope:
            ql = sb("ql", [P, 2, 2, TOK], scope=scope)
            pr = sb("mpr", [P, 2, LP], scope=scope)
            PT = sb("mPT", [P, 2, NT, LP], scope=scope)
            ol = sb("ol", [P, 2, LP], scope=scope)
            stat = sb("mstat", [P, 2, 3], scope=scope)
            with nc.Block() as block:
                @block.sync
                def _(sp):
                    for src, name in ((ctok, "c_latent"), (kpetok, "c_kpe")):
                        pr_, s = out[name + "_p"][0, 0], out[name + "_s"][0, :, 0]
                        store(sp, pr_[0:4 * P].rearrange("(t p) n -> p t n", p=P), src[:, 0:4])
                        store(sp, pr_[4 * P:], src[:META, 4])
                        store(sp, s, src[META:META + NS, 4])
                    sp.wait_ge(out_done, 16 * outs[0])

                @block.tensor
                def _(pe):
                    def run_task(q):
                        kind, h, k = tasks[q]
                        if q:
                            pe.wait_ge(mla_evac, q)
                        if kind == "query":
                            r = slice(64 * (h % 2), 64 * (h % 2) + 64)
                            for s in range(2):
                                mm = nc.tensor.matmul(PS[3][:, 512 * s:512 * s + HALF], ukT[r, h // 2, k],
                                                      qnT[r, h // 2, s * HALF:(s + 1) * HALF], start=True, stop=True)
                        elif kind == "latent":
                            pe.wait_ge(at_ptc, A0 + NT * (h + 1))
                            for kt in range(NT):
                                m = rows_of(kt)
                                for bank, a, b in ((0, 0, 256), (256, 256, LP)):
                                    q0 = max(a, P * kt)
                                    if q0 < b:
                                        mm = nc.tensor.matmul(PS[3][:, bank + q0:bank + b], ctok[:m, kt, k * P:(k + 1) * P],
                                                              PT[:m, h % 2, kt, q0:b], start=kt == 0, stop=kt == NT - 1,
                                                              skip_group_check=True)
                        else:
                            for c in range(2):
                                for bank, a, b in ((0, 0, 256), (256, 256, LP)):
                                    mm = nc.tensor.matmul(PS[3][:, bank + a:bank + b], uv[:, c, h], ol[:, c, a:b],
                                                          start=c == 0, stop=c == 1)
                        mm.then_inc(mla_task, 1)

                    def logits(i):
                        h, t = pairs[i]
                        n, w, e = rows_of(t), width(t), ROPE * (h % 4)
                        if i >= 2:
                            pe.wait_ge(at_exp, A0 + i - 1)
                        for a, b in ((0, min(w, 512)), (512, w)):
                            if b > a:
                                for c in range(2):
                                    nc.tensor.matmul(PS[i % 2][:n, a:b], ql[:, h % 2, c, P * t:P * t + n], cT[:, c, a:b],
                                                     start=c == 0, stop=False)
                                mm = nc.tensor.matmul(PS[i % 2][:n, a:b], qpT[e:e + ROPE, h // 4, P * t:P * t + n],
                                                      kpeT[e:e + ROPE, a:b], start=False, stop=True)
                        mm.then_inc(at_qk, 1)

                    for q in due[-1]:
                        run_task(q)
                    pe.wait_ge(mla_evac, 2)
                    logits(0)
                    for i, (h, t) in enumerate(pairs):
                        if i + 1 < NP:
                            if t == NT - 1:
                                pe.wait_ge(mla_evac, due[i - 1][-1] + 1)
                            logits(i + 1)
                        n = rows_of(t)
                        pe.wait_ge(at_p, A0 + i + 1)
                        if i:
                            pe.wait_ge(at_ptc, A0 + i)
                        for kt in range(t + 1):
                            m = rows_of(kt)
                            mm = nc.tensor.transpose(PS[2][:m, P * kt:P * kt + n], pr[:n, i % 2, P * kt:P * kt + m],
                                                     cst["ident"][:n, :n])
                        mm.then_inc(at_pt, 1)
                        for q in due.get(i, []):
                            run_task(q)
                    for q in due[NP]:
                        run_task(q)

                @block.scalar
                def _(act):
                    def evacuate(q):
                        kind, h, k = tasks[q]
                        act.wait_ge(mla_task, q + 1)
                        if kind == "query":
                            nc.scalar.activation(halves(ql[:, h % 2, k]), halves(PS[3][:, :])[:, :, :HALF], ACT.Copy)
                            ins = nc.scalar.activation(qlS[:, k, :, h], PS[3][:, 512 + HALF - NS:512 + HALF], ACT.Copy)
                        else:
                            dst = ol[:, k] if kind == "latent" else oT[:, h]
                            nc.scalar.activation(dst[:, 0:256], PS[3][:, 0:256], ACT.Copy)
                            ins = nc.scalar.activation(dst[:, 256:LP], PS[3][:, 512:784], ACT.Copy)
                        ins.then_inc(mla_evac, 1)

                    def copy_pt(i):
                        h, t = pairs[i]
                        n, c = rows_of(t), P * t
                        act.wait_ge(at_pt, A0 + i + 1)
                        if h >= 2 and t == 0:
                            act.wait_ge(mla_task, tasks.index(("latent", h - 2, 1)) + 1)
                        full = min(t + 1, 4)
                        ins = nc.scalar.activation(PT[:, h % 2, 0:full, c:c + n],
                                                   PS[2][:, 0:512].rearrange("p (k n) -> p k n", k=4)[:, :full, :n], ACT.Copy)
                        if t == NT - 1:
                            ins = nc.scalar.activation(PT[:META, h % 2, 4, c:c + n], PS[2][:META, 512:512 + n], ACT.Copy)
                        ins.then_inc(at_ptc, 1)

                    for q in due[-1]:
                        evacuate(q)
                    for i, (h, t) in enumerate(pairs):
                        n, w = rows_of(t), width(t)
                        act.wait_ge(at_max, A0 + i + 1)
                        if i >= 2:
                            act.wait_ge(at_pt, A0 + i - 1)
                        nc.scalar.activation(pr[:n, i % 2, :w], PS[i % 2][:n, :w], ACT.Exp, bias=stat[:n, i % 2, 0:1],
                                             accum_out=stat[:n, i % 2, 1:2]).then_inc(at_exp, 1)
                        if i:
                            copy_pt(i - 1)
                            for q in due.get(i - 1, []):
                                evacuate(q)
                    copy_pt(NP - 1)
                    for q in due.get(NP - 1, []) + due[NP]:
                        evacuate(q)

                @block.vector
                def _(dve):
                    link = chain_dve.link

                    def normalise(i):
                        h, t = pairs[i]
                        n, w = rows_of(t), width(t)
                        dve.wait_ge(at_exp, A0 + i + 1)
                        link(dve, nc.vector.reciprocal(stat[:n, i % 2, 2:3], stat[:n, i % 2, 1:2]))
                        nc.vector.tensor_scalar(pr[:n, i % 2, :w], pr[:n, i % 2, :w], stat[:n, i % 2, 2:3], None, ALU.mult)\
                            .then_inc(at_p, 1)

                    for i, (h, t) in enumerate(pairs):
                        n, w = rows_of(t), width(t)
                        dve.wait_ge(at_qk, A0 + i + 1)
                        diag = PS[i % 2][:n, P * t:P * t + n]
                        link(dve, nc.vector.tensor_tensor(diag, diag, cst["tri"][:n, :n], ALU.add))
                        nc.vector.tensor_reduce(stat[:n, i % 2, 0:1], PS[i % 2][:n, :w], AXX, ALU.max, negate=True)\
                            .then_inc(at_max, 1)
                        if i:
                            normalise(i - 1)
                    normalise(NP - 1)
        LQ.close()

        NCX = 12
        STEPS = 2 * G
        cx_ps, cx_ca, cx_cd, sx_ps, sx_max, sx_exp, sx_pt, sx_ptc, sx_pv, sx_o = (
            sem(n) for n in ("cx_ps", "cx_ca", "cx_cd", "sx_ps", "sx_max", "sx_exp", "sx_pt", "sx_ptc", "sx_pv", "sx_o"))
        cx_sem = kx_sem + [sem(f"cx_in{i}") for i in range(NKX, NCX)]
        cx_base = [16 * (NS * G // NKX)] * NKX + [0] * (NCX - NKX)
        with ExitStack() as scope:
            cx = sb("cx", [P, NCX, 4 * KV], scope=scope)
            px = sb("px", [P, NCX, 4 * ROPE], scope=scope)
            cxT = sb("cxT", [P, 4, 2, 512], scope=scope)
            pxT = sb("pxT", [P, 4, P], scope=scope)
            prob = sb("prob", [P, 512], scope=scope)
            probT = sb("probT", [P, 4, P], scope=scope)
            top = sb("top", [P, 2, G + 1], scope=scope)
            ntop, corr, part_sum = (sb(n, [P, STEPS], scope=scope) for n in ("ntop", "corr", "part_sum"))
            total = sb("total", [P, 2, G + 1], scope=scope)
            acc = sb("acc", [P, 2, KV], scope=scope)
            inv = sb("inv", [P, 2], scope=scope)
            olS = sb("olS", [P, 2, H, NS], scope=scope)
            qp4 = cconst[:, 0:4 * NS * 32].rearrange("p (s b h) -> p s b h", s=4, b=NS)

            with nc.Block() as block:
                @block.gpsimd
                def _(pool):
                    src_c = d["cache_c_latent"][0].rearrange("n (r s) e -> (n r) (s e)", s=4)
                    src_p = d["cache_c_kpe"][0].rearrange("n (r s) e -> (n r) (s e)", s=4)
                    for k in range(STEPS):
                        half, g = k // G, k % G
                        if k * 4 >= NCX:
                            pool.wait_ge(sx_pv, k - NCX // 4 + 1)
                        for j in range(4):
                            i = (4 * k + j) % NCX
                            c = G * (4 * half + j) + g
                            off = bass.IndirectOffsetOnAxis(ap=page_idx[:, c:c + 1], axis=0)
                            pool.indirect_dma_start(cx[:, i], None, src_c, off).then_inc(cx_sem[i], 16)
                            pool.indirect_dma_start(px[:, i], None, src_p, off).then_inc(cx_sem[i], 16)

                @block.tensor
                def _(pe):
                    ident = cst["ident"]
                    pe.wait_ge(lat_act, 5)
                    for half in range(2):
                        for j in range(4):
                            b, rows_ = 4 * half + j, slice(32 * j, 32 * j + 32)
                            o = PS[1][rows_, 512 + half:513 + half]
                            for c in range(2):
                                nc.tensor.matmul(o, qlS[:, c, b, :], cT[:, c, LP + b:LP + b + 1], start=c == 0, stop=False,
                                                 tile_position=(0, 32 * j))
                            nc.tensor.matmul(o, qp4[:, 0, b, :], kpeT[:, LP + b:LP + b + 1], start=False, stop=True,
                                             tile_position=(0, 32 * j))
                    for half in range(2):
                        mm = nc.tensor.matmul(PS[1][:, KV * half:KV * half + KV], cc["bsel"][0:META + NS, P * half:P * half + P],
                                              ctok[0:META + NS, 4, :], start=True, stop=True)
                    mm.then_inc(lat_pe, 1)
                    for k in range(STEPS + 1):
                        half = k // G
                        if k < STEPS:
                            for j in range(4):
                                i = (4 * k + j) % NCX
                                turn = (4 * k + j) // NCX + 1
                                pe.wait_ge(cx_sem[i], cx_base[i] + 32 * turn)
                                bank = j % 2
                                if k == 0 and j == 1:
                                    pe.wait_ge(lat_dve, 3)
                                if 4 * k + j >= 2:
                                    pe.wait_ge(cx_ca if bank == 0 else cx_cd, 2 * k + j // 2 + (k if bank == 0 else 0))
                                for c in range(2):
                                    for s in range(4):
                                        nc.tensor.transpose(PS[bank][:, 512 * c + P * s:512 * c + P * s + P],
                                                            cx[:, i, KV * s + P * c:KV * s + P * c + P], ident)
                                mm = nc.tensor.transpose(PS[3][:, P * j:P * j + P], px[:, i], ident)
                                mm.then_inc(cx_ps, 1)
                        if k:
                            pe.wait_ge(sx_exp, k)
                            for s in range(4):
                                mm = nc.tensor.transpose(PS[2][:, 512 + P * s:512 + P * s + P], prob[:, P * s:P * s + P], ident)
                            mm.then_inc(sx_pt, 1)
                        if k < STEPS:
                            pe.wait_ge(cx_ca, 3 * k + 3)
                            pe.wait_ge(cx_cd, 2 * k + 2)
                            for s in range(4):
                                for j in range(4):
                                    nc.tensor.matmul(PS[2][32 * j:32 * j + 32, P * s:P * s + P], qp4[:, s, 4 * half + j, :],
                                                     pxT[:, j], start=s == 0, stop=False, tile_position=(0, 32 * j),
                                                     skip_group_check=True)
                            for c in range(2):
                                for j in range(4):
                                    mm = nc.tensor.matmul(PS[2][32 * j:32 * j + 32, 0:512], qlS[:, c, 4 * half + j, :], cxT[:, j, c],
                                                          start=False, stop=c == 1, tile_position=(0, 32 * j),
                                                          skip_group_check=True)
                            mm.then_inc(sx_ps, 1)
                        if k:
                            pe.wait_ge(sx_ptc, k)
                            if k >= 2:
                                pe.wait_ge(sx_o, k - 1)
                            for s in range(4):
                                for j in range(4):
                                    i = (4 * (k - 1) + j) % NCX
                                    mm = nc.tensor.matmul(PS[3][32 * j:32 * j + 32, 512:512 + KV], probT[:, s, 32 * j:32 * j + 32],
                                                          cx[:, i, KV * s:KV * s + KV], start=s == 0, stop=s == 3,
                                                          tile_position=(0, 32 * j))
                            mm.then_inc(sx_pv, 1)
                    pe.wait_ge(lat_dve, 4)
                    for half in range(2):
                        for c in range(2):
                            mm = nc.tensor.transpose(PS[0][:, P * (2 * half + c):P * (2 * half + c + 1)],
                                                     acc[:, half, P * c:P * c + P], ident)
                    mm.then_inc(lat_pe, 1)
                    pe.wait_ge(lat_act, 6)
                    for h in range(H):
                        for c in range(2):
                            mm = nc.tensor.matmul(PS[1][:, NS * h:NS * h + NS], uv[:, c, h], olS[:, c, h], start=c == 0, stop=c == 1)
                    mm.then_inc(lat_pe, 1)

                @block.scalar
                def _(act):
                    act.wait_ge(lat_dve, 2)
                    for s in range(4):
                        r = slice(ROPE * s, ROPE * s + ROPE)
                        ins = nc.scalar.activation(qp4[r, s], qpS[r], ACT.Copy)
                    ins.then_inc(lat_act, 1)
                    for k in range(STEPS + 1):
                        if k < STEPS:
                            for j in (0, 2):
                                act.wait_ge(cx_ps, 4 * k + j + 1)
                                nc.scalar.activation(cxT[:, j].rearrange("p c n -> p (c n)"), PS[0][:, :], ACT.Copy).then_inc(cx_ca, 1)
                            act.wait_ge(cx_ps, 4 * k + 4)
                            nc.scalar.activation(pxT[:, :, :].rearrange("p j n -> p (j n)"), PS[3][:, 0:512], ACT.Copy)\
                                .then_inc(cx_ca, 1)
                        if k:
                            act.wait_ge(sx_pt, k)
                            nc.scalar.activation(probT[:, :, :].rearrange("p s n -> p (s n)"), PS[2][:, 512:1024], ACT.Copy)\
                                .then_inc(sx_ptc, 1)
                        if k < STEPS:
                            half, g = k // G, k % G
                            act.wait_ge(sx_max, k + 1)
                            nc.scalar.activation(corr[:, k:k + 1], top[:, half, g:g + 1], ACT.Exp, bias=ntop[:, k:k + 1])
                            nc.scalar.activation(prob[:, :], PS[2][:, 0:512], ACT.Exp, bias=ntop[:, k:k + 1],
                                                 accum_out=part_sum[:, k:k + 1]).then_inc(sx_exp, 1)
                    act.wait_ge(lat_pe, 6)
                    for half in range(2):
                        for c in range(2):
                            src = PS[0][:, P * (2 * half + c):P * (2 * half + c + 1)].rearrange("p (j h) -> p h j", j=4)[:, 0:H]
                            ins = nc.scalar.activation(olS[:, c, :, 4 * half:4 * half + 4], src, ACT.Copy)
                    ins.then_inc(lat_act, 1)
                    act.wait_ge(lat_pe, 7)
                    nc.scalar.activation(oT[:, :, LP:], PS[1][:, 0:NS * H].rearrange("p (h b) -> p h b", h=H), ACT.Copy)\
                        .then_inc(lat_act, 1)

                @block.vector
                def _(dve):
                    link = chain_dve.link
                    nc.vector.memset(qp4[:, :, :, :], 0.0).then_inc(lat_dve, 1)
                    dve.wait_ge(lat_pe, 5)
                    nc.vector.tensor_copy(top[:, :, 0], PS[1][:, 512:514])
                    nc.vector.memset(total[:, :, 0], 1.0)
                    nc.vector.tensor_copy(acc[:, :, :].rearrange("p a n -> p (a n)"), PS[1][:, 0:2 * KV]).then_inc(lat_dve, 1)
                    dve.wait_ge(lat_dve, 3)
                    for k in range(STEPS + 1):
                        if k < STEPS:
                            half, g = k // G, k % G
                            for j in (1, 3):
                                dve.wait_ge(cx_ps, 4 * k + j + 1)
                                nc.vector.tensor_copy(cxT[:, j].rearrange("p c n -> p (c n)"), PS[1][:, :]).then_inc(cx_cd, 1)
                            dve.wait_ge(sx_ps, k + 1)
                            new = top[:, half, g + 1:g + 2]
                            link(dve, nc.vector.tensor_reduce(new, PS[2][:, 0:512], AXX, ALU.max))
                            link(dve, nc.vector.tensor_tensor(new, new, top[:, half, g:g + 1], ALU.max))
                            nc.vector.tensor_scalar(ntop[:, k:k + 1], new, -1.0, None, ALU.mult).then_inc(sx_max, 1)
                        if k:
                            half, g = (k - 1) // G, (k - 1) % G
                            dve.wait_ge(sx_exp, k)
                            link(dve, nc.vector.scalar_tensor_tensor(total[:, half, g + 1:g + 2], total[:, half, g:g + 1],
                                                                     corr[:, k - 1:k], part_sum[:, k - 1:k], ALU.mult, ALU.add))
                            dve.wait_ge(sx_pv, k)
                            nc.vector.scalar_tensor_tensor(acc[:, half], acc[:, half], corr[:, k - 1:k], PS[3][:, 512:512 + KV],
                                                           ALU.mult, ALU.add).then_inc(sx_o, 1)
                            dve.wait_ge(sx_o, k)
                    link(dve, nc.vector.reciprocal(inv[:, :], total[:, :, G]))
                    nc.vector.tensor_tensor(acc[:, :, :], acc[:, :, :], inv[:, :].unsqueeze(2).to_broadcast([P, 2, KV]), ALU.mult)\
                        .then_inc(lat_dve, 1)
        L1.close()

        with ExitStack() as scope:
            x_hi, x_lo = sb("x_hi", [P, KT, TOK], F32R, scope), sb("x_lo", [P, KT, TOK], F32R, scope)
            lo_before = count["tile"]
            sp_act, sp_dve = split(oT, KT, x_hi, x_lo)
            out_projection(JO1, x_hi, x_lo, sp_act, sp_dve, FFN2, 0)
            hid_hi, hid_lo = sb("hid_hi", [P, KT, TOK], F32R, scope), sb("hid_lo", [P, KT, TOK], F32R, scope)
            mlp(1, JM1, x_hi, x_lo, hid_hi, hid_lo, 0)
        with ExitStack() as scope:
            yT = sb("yT", [P, KT, TOK], scope=scope)
            ytok = sb("ytok", [P, NT, D], scope=scope)
            n_act, n_pe, n_dve = norm(hT, KT, D, FINAL, None, None, keep=yT)
            y_ready = count["normed"]
            with nc.Block() as block:
                @block.scalar
                def _(act):
                    n_act(act)
                    for t in range(NT):
                        n = P if t < 4 else META + NS
                        act.wait_ge(xt_ready, KT + 1 + t + 1)
                        nc.scalar.activation(ytok[:n, t], PS[t % 2][:n, :], ACT.Copy).then_inc(x_out, 1)

                @block.vector
                def _(dve):
                    n_dve(dve)

                @block.tensor
                def _(pe):
                    n_pe(pe)
                    pe.wait_ge(normed, y_ready)
                    for t in range(NT):
                        n = P if t < 4 else META + NS
                        if t >= 2:
                            pe.wait_ge(x_out, KT + 1 + t - 1)
                        for k in range(KT):
                            mm = nc.tensor.transpose(PS[t % 2][:n, k * P:k * P + P], yT[:, k, t * P:t * P + n], cst["ident"])
                        mm.then_inc(xt_ready, 1)

                @block.sync
                def _(sp):
                    y = out["y_prompt"][0]
                    for t in range(NT):
                        sp.wait_ge(x_out, KT + 1 + t + 1)
                        a, b = (META if t == 0 else 0), (P if t < 4 else META)
                        store(sp, y[t * P - META + a:t * P - META + b], ytok[a:b, t])
                    store(sp, out["y_sample"][:, 0], ytok[META:META + NS, 4])
                    for n in range(len(jobs) - NRAW, len(jobs)):
                        sp.wait_ge(raw_in[n % NRAW], raw_count[n])
                    sp.wait_ge(out_done, 16 * outs[0])


_IN = ("x_prompt", "x_sample", "state_a_conv", "state_a_ssm", "cache_b_k", "cache_b_v", "cache_b_kidx", "cache_c_latent",
       "cache_c_kpe", "page_table", "meta_tokens", "rel_bias", "norm_mix", "norm_ffn", "norm_final", "w_in_ab", "conv_a",
       "a_log", "dt_bias_a", "gnorm_a", "w_out_ab", "w_in_c", "qnorm_c", "kvnorm_c", "w_uq_c", "w_uk_c", "w_uv_c",
       "w_out_c", "w_up", "w_down")
_OUT = (("y_prompt", (1, SEQ, D)), ("y_sample", (NS, 1, D)),
        ("a_conv_p", (1, 1, 3, QKV)), ("a_ssm_p", (1, 1, H, DH, DH)), ("b_k_p", (1, 1, LP, H, DH)),
        ("b_v_p", (1, 1, LP, H, DH)), ("b_kidx_p", (1, 1, LP, DH)), ("c_latent_p", (1, 1, LP, KV)),
        ("c_kpe_p", (1, 1, LP, ROPE)),
        ("a_conv_s", (1, NS, 3, QKV)), ("a_ssm_s", (1, NS, H, DH, DH)), ("b_k_s", (1, NS, 1, H, DH)),
        ("b_v_s", (1, NS, 1, H, DH)), ("b_kidx_s", (1, NS, 1, DH)), ("c_latent_s", (1, NS, 1, KV)),
        ("c_kpe_s", (1, NS, 1, ROPE)))


def kernel(**inputs):
    import numpy as _np
    import concourse.bacc as _bacc
    from concourse import mybir as _mybir
    from concourse.bass_utils import run_bass_kernel_spmd as _run

    arrays = {name: _np.ascontiguousarray(inputs[name]) for name in _IN}
    c, masks, onehot = constants()
    arrays["consts"] = _np.concatenate([c[n] for n, _ in CONST_COLS], 1)
    arrays["masks"], arrays["onehot"] = masks, onehot
    arrays.update(more_constants())
    arrays.update(rope_constants())
    nc = _bacc.Bacc("TRN2", target_bir_lowering=False, num_devices=1)
    d = {k: nc.dram_tensor("in_" + k, v.shape, _mybir.dt.from_np(v.dtype), kind="ExternalInput").ap()
         for k, v in arrays.items()}
    out = {k: nc.dram_tensor("out_" + k, s, _mybir.dt.float32, kind="ExternalOutput").ap() for k, s in _OUT}
    trunk(nc, d, out)
    r = _run(nc, [{"in_" + k: v for k, v in arrays.items()}], core_ids=[0])
    return tuple(r.results[0]["out_" + k] for k, _ in _OUT)
```
